# Optimizing a Trainium2 kernel written in Bass

```python
import jax, jax.numpy as jnp
from jax import lax
import numpy as np

D_MODEL = 1024
BATCH = 1
SEQ = 2048
DEPTH = 1

MEM_LEN = 256
N_MIXERS = 2
CHUNK = 64
NORM_EPS = 1e-6
GLA_HEADS = 4
GLA_DK = (D_MODEL // 2) // GLA_HEADS
GLA_DV = D_MODEL // GLA_HEADS
GLA_GATE_RANK = 16
GLA_TAU = 16.0
HGRN_EXPAND = 128
HGRN_HEADS = D_MODEL // HGRN_EXPAND
HGRN_DF = HGRN_EXPAND
HGRN_FDIM = HGRN_HEADS * HGRN_DF
HGRN_DI = D_MODEL // HGRN_HEADS
XA_HEADS = 4
XA_DH = 128
XA_DIM = XA_HEADS * XA_DH
MLP_HIDDEN = 4 * D_MODEL
MIX_OUT_DIM = D_MODEL + XA_DIM
GLA_SPLITS = (GLA_HEADS * GLA_DK, GLA_HEADS * GLA_DK, GLA_HEADS * GLA_DV, GLA_GATE_RANK, D_MODEL, XA_DIM)
HGRN_SPLITS = (HGRN_FDIM, HGRN_FDIM, D_MODEL, D_MODEL, XA_DIM)
GLA_IN_DIM = sum(GLA_SPLITS)
HGRN_IN_DIM = sum(HGRN_SPLITS)

kernel_name = "hybrid_gla_hgrn2_memxattn_sqrelu"

def rms_norm(x, gain):
    x32 = x.astype(jnp.float32)
    y = x32 * lax.rsqrt(jnp.mean(x32 * x32, axis=-1, keepdims=True) + NORM_EPS)
    return (y * gain.astype(jnp.float32)).astype(x.dtype)

def split_cols(a, sizes):
    idx = [int(v) for v in np.cumsum(sizes)[:-1]]
    return jnp.split(a, idx, axis=-1)

def chunked_gated_linear_attention(q, k, v, log_decay):
    B, T, H, dk = q.shape
    dv = v.shape[-1]
    n = T // CHUNK

    def to_chunks(a):
        return a.astype(jnp.float32).reshape(B, n, CHUNK, H, a.shape[-1]).transpose(1, 0, 3, 2, 4)

    causal = jnp.tril(jnp.ones((CHUNK, CHUNK), dtype=bool))[None, None, :, :, None]

    def step(S, inp):
        qb, kb, vb, gb = inp
        b = jnp.cumsum(gb, axis=2)
        rel = jnp.exp(jnp.where(causal, b[:, :, :, None, :] - b[:, :, None, :, :], -jnp.inf))
        attn = jnp.einsum('bhtd,bhsd,bhtsd->bhts', qb, kb, rel)
        o = (jnp.einsum('bhtd,bhdv->bhtv', qb * jnp.exp(b), S)
             + jnp.einsum('bhts,bhsv->bhtv', attn, vb))
        b_last = b[:, :, -1, :]
        S = (jnp.exp(b_last)[..., None] * S
             + jnp.einsum('bhsd,bhsv->bhdv', kb * jnp.exp(b_last[:, :, None, :] - b), vb))
        return S, o

    S0 = jnp.zeros((B, H, dk, dv), jnp.float32)
    _, o = lax.scan(step, S0, (to_chunks(q), to_chunks(k), to_chunks(v), to_chunks(log_decay)))
    return o.transpose(1, 0, 3, 2, 4).reshape(B, T, H, dv)

def gla_branch(h, w_in, w_gate2, b_gate, out_gain):
    B, T, _ = h.shape
    q, k, v, g_lr, r, xq = split_cols(h @ w_in, GLA_SPLITS)
    q = q.reshape(B, T, GLA_HEADS, GLA_DK) * (GLA_DK ** -0.5)
    k = k.reshape(B, T, GLA_HEADS, GLA_DK)
    v = v.reshape(B, T, GLA_HEADS, GLA_DV)
    z = (g_lr @ w_gate2 + b_gate).astype(jnp.float32)
    log_alpha = (jax.nn.log_sigmoid(z) / GLA_TAU).reshape(B, T, GLA_HEADS, GLA_DK)
    o = chunked_gated_linear_attention(q, k, v, log_alpha)
    o = rms_norm(o, out_gain) * jax.nn.silu(r.astype(jnp.float32)).reshape(B, T, GLA_HEADS, GLA_DV)
    return o.reshape(B, T, D_MODEL).astype(h.dtype), xq

def hgrn2_branch(h, w_in, lower_bound, out_gain):
    B, T, _ = h.shape
    q, f, i, g, xq = split_cols(h @ w_in, HGRN_SPLITS)
    q = jax.nn.silu(q).reshape(B, T, HGRN_HEADS, HGRN_DF) * (HGRN_DF ** -0.5)
    lb = lower_bound.astype(jnp.float32)
    forget = lb + (1.0 - lb) * jax.nn.sigmoid(f.astype(jnp.float32))
    k = (1.0 - forget).reshape(B, T, HGRN_HEADS, HGRN_DF)
    log_f = jnp.log(forget).reshape(B, T, HGRN_HEADS, HGRN_DF)
    i = i.reshape(B, T, HGRN_HEADS, HGRN_DI)
    o = chunked_gated_linear_attention(q, k, i, log_f)
    o = rms_norm(o, out_gain) * jax.nn.silu(g.astype(jnp.float32)).reshape(B, T, HGRN_HEADS, HGRN_DI)
    return o.reshape(B, T, D_MODEL).astype(h.dtype), xq

def memory_cross_attention(xq, m, w_kv):
    B, T, _ = xq.shape
    km, vm = split_cols(m @ w_kv, (XA_DIM, XA_DIM))
    qh = xq.reshape(B, T, XA_HEADS, XA_DH)
    km = km.reshape(B, -1, XA_HEADS, XA_DH)
    vm = vm.reshape(B, -1, XA_HEADS, XA_DH)
    scores = jnp.einsum('bthd,bmhd->bhtm', qh, km).astype(jnp.float32) * (XA_DH ** -0.5)
    p = jax.nn.softmax(scores, axis=-1).astype(vm.dtype)
    out = jnp.einsum('bhtm,bmhd->bthd', p, vm)
    return out.reshape(B, T, XA_DIM)

def sq_relu_mlp(h, w_up, w_down):
    u = jax.nn.relu(h @ w_up)
    return (u * u) @ w_down

def setup_inputs(seed: int = 0) -> dict:
    key = jax.random.key(seed)
    ks = jax.random.split(key, 20)
    n_gla = len(range(0, DEPTH, N_MIXERS))
    n_hgrn = len(range(1, DEPTH, N_MIXERS))
    f32 = jnp.float32

    def w(k, shape, fan_in):
        return jax.random.normal(k, shape, f32) * (fan_in ** -0.5)

    def gain(k, shape):
        return 1.0 + 0.02 * jax.random.normal(k, shape, f32)

    return {
        "x": jax.random.normal(ks[0], (BATCH, SEQ, D_MODEL), f32),
        "mem": jax.random.normal(ks[1], (BATCH, MEM_LEN, D_MODEL), f32),
        "norm_mix": gain(ks[2], (DEPTH, D_MODEL)),
        "norm_mem": gain(ks[3], (DEPTH, D_MODEL)),
        "w_kv": w(ks[4], (DEPTH, D_MODEL, 2 * XA_DIM), D_MODEL),
        "w_out": w(ks[5], (DEPTH, MIX_OUT_DIM, D_MODEL), MIX_OUT_DIM),
        "norm_mlp": gain(ks[6], (DEPTH, D_MODEL)),
        "w_up": w(ks[7], (DEPTH, D_MODEL, MLP_HIDDEN), D_MODEL),
        "w_down": w(ks[8], (DEPTH, MLP_HIDDEN, D_MODEL), MLP_HIDDEN),
        "gla_w_in": w(ks[9], (n_gla, D_MODEL, GLA_IN_DIM), D_MODEL),
        "gla_w_gate2": w(ks[10], (n_gla, GLA_GATE_RANK, GLA_HEADS * GLA_DK), GLA_GATE_RANK),
        "gla_b_gate": 0.1 * jax.random.normal(ks[11], (n_gla, GLA_HEADS * GLA_DK), f32),
        "gla_out_gain": gain(ks[12], (n_gla, GLA_DV)),
        "hgrn_w_in": w(ks[13], (n_hgrn, D_MODEL, HGRN_IN_DIM), D_MODEL),
        "hgrn_lower_bounds": 0.1 * jax.random.normal(ks[14], (DEPTH, HGRN_FDIM), f32),
        "hgrn_out_gain": gain(ks[15], (n_hgrn, HGRN_DI)),
        "final_norm": gain(ks[16], (D_MODEL,)),
    }

def reference(x, mem, norm_mix, norm_mem, w_kv, w_out, norm_mlp, w_up, w_down,
              gla_w_in, gla_w_gate2, gla_b_gate, gla_out_gain,
              hgrn_w_in, hgrn_lower_bounds, hgrn_out_gain, final_norm):
    p = jax.nn.softmax(hgrn_lower_bounds.astype(jnp.float32), axis=0)
    lower_bounds = jnp.cumsum(p, axis=0) - p[0]

    for i in range(DEPTH):
        j = i // N_MIXERS
        h = rms_norm(x, norm_mix[i])
        m = rms_norm(mem, norm_mem[i])
        if i % N_MIXERS == 0:
            y_mix, xq = gla_branch(h, gla_w_in[j], gla_w_gate2[j], gla_b_gate[j], gla_out_gain[j])
        else:
            y_mix, xq = hgrn2_branch(h, hgrn_w_in[j], lower_bounds[i], hgrn_out_gain[j])
        y_mem = memory_cross_attention(xq, m, w_kv[i])
        x = x + jnp.concatenate([y_mix, y_mem.astype(y_mix.dtype)], axis=-1) @ w_out[i]
        x = x + sq_relu_mlp(rms_norm(x, norm_mlp[i]), w_up[i], w_down[i])
    return rms_norm(x, final_norm)


_drawn_inputs = setup_inputs


def setup_inputs(seed=0):
    import zlib

    import numpy as np

    out = dict(_drawn_inputs(seed))
    spreads = {}
    factors = {'norm_mix': 2.81,
     'norm_mem': 8.0,
     'norm_mlp': 9.997,
     'gla_out_gain': 18.874,
     'final_norm': 8.103}
    for name, (base, spread) in spreads.items():
        noise = np.random.default_rng([zlib.crc32(name.encode()), seed]).standard_normal(out[name].shape)
        drawn = base * np.exp(spread * noise) if base else spread * noise
        out[name] = __import__('jax').numpy.asarray(drawn.astype(out[name].dtype))
    for name, factor in factors.items():
        out[name] = (out[name] * factor).astype(out[name].dtype)
    return out
```

```python
from contextlib import ExitStack

import numpy as np

import concourse.bass as bass
from concourse import mybir

F32 = mybir.dt.float32
F32R = mybir.dt.float32r
BF16 = mybir.dt.bfloat16
U8 = mybir.dt.uint8
ALU = mybir.AluOpType
ACT = mybir.ActivationFunctionType
AX_X = mybir.AxisListType.X

P = 128
D = 1024
KD = D // P
SEQ = 2048
BLOCK = 512
BLOCKS = SEQ // BLOCK
TILES = BLOCK // P
MEM = 256
MT = MEM // P
HEADS = 4
DK = 128
DV = 256
RANK = 16
TAU = 16.0
XH = 4
XD = XH * P
HIDDEN = 4 * D
EPS = 1e-6
QSCALE = DK ** -0.5
XSCALE = P ** -0.5

COL_Q = 0
COL_K = COL_Q + HEADS * DK
COL_V = COL_K + HEADS * DK
COL_G = COL_V + HEADS * DV
COL_R = COL_G + RANK
COL_XQ = COL_R + D

WIDTHS = [64, 32, 16, 8, 4, 2, 1]
HALF = P // 2
LEVELS = len(WIDTHS) + 1
QUERY_DECAY = len(WIDTHS)
KEY_DECAY = QUERY_DECAY + 1
DECAYS = KEY_DECAY + 1

CHUNK = 2048
FCOLS = CHUNK // KD
KG = 4
C_XQ, C_Q, C_K, C_V, C_R = 0, 2, 4, 6, 10
C_OUT = C_R + 4
OUT_ORDER = (2, 0, 1)
C_UP = [C_OUT + 6, C_OUT + 6 + 16]
C_DOWN = [C_UP[0] + 8, C_UP[1] + 8]
CHUNKS = C_DOWN[1] + 8
KV_CHUNKS = 4
HALF_HIDDEN = HIDDEN // 2
UF = HALF_HIDDEN // P
STEPS = 2 * (C_OUT - C_V)


class Signal:

    def __init__(self, sem, before, per_block, step=1):
        self.sem, self.before, self.per_block, self.step = sem, before, per_block, step

    def at(self, n, k):
        return self.sem, n * (self.per_block * self.step) + (self.before + k + 1) * self.step

    def early(self, k):
        return self.sem, (k + 1) * self.step


class UseOrder:

    def __init__(self, uses):
        self.count = [0] * 8
        self.place = {}
        for bank, name in uses:
            self.place[name] = (bank, self.count[bank])
            self.count[bank] += 1


def early_uses():
    for k in range(KD):
        yield (6, 7, 4, 5)[k % 4], ("memT", k)
    for h in range(XH):
        yield h % 2, ("km", h)
    for c in range(2):
        for m in range(MT):
            yield 2 + m, ("vm", c, m)
    for k in range(KD):
        yield (6, 7, 4, 5)[k % 4], ("x0T", k)


def block_uses():
    for h in range(XH):
        yield h % 2, ("xq", h)
    yield 2, "g"
    for h in range(HEADS):
        yield (4, 5, 3, 2)[h], ("z", h)
    for f in range(4):
        yield f % 2, ("q", f)
        if f % 2:
            for use in attention_uses(C_Q + f // 2):
                yield use
    for f in range(4):
        yield f % 2, ("k", f)
        if f % 2 == 0:
            for p in range(2):
                yield 4 + p, ("pv", f // 2, p)
        else:
            for use in attention_uses(C_K + f // 2):
                yield use
    for hs in range(STEPS):
        if hs < 8:
            if hs // 2 % 2 == 0:
                for t in (2 * (hs % 2), 2 * (hs % 2) + 1):
                    yield 2 + t, ("v", hs // 4, t)
        else:
            yield hs % 2, ("r", hs - 8)
        if hs == 0:
            for p in range(2):
                yield 6 + p, ("pT", TILES - 1, p)
        if hs in (0, 2):
            for p in range(2):
                yield p, ("pv", 2 + hs // 2, p)
        for level in levels_of(hs):
            yield 6 + level % 2, ("level", hs // 4, level)
        for what, c in STATE_STEPS.get(hs, ()):
            for use in state_uses(what, c):
                yield use
    for what, c in (("o", 3), ("kT", 3), ("oT", (0, 0)), ("oT", (1, 0)), ("oT", (2, 0)), ("oT", (3, 0)), ("su", 3),
                    ("oT", (0, 1)), ("oT", (1, 1)), ("oT", (2, 1)), ("oT", (3, 1))):
        for use in state_uses(what, c):
            yield use
    for d in range(2):
        for t in range(TILES):
            yield 2 + t, ("out", d, t)
    for g in range(KD // 2):
        yield (6, 7, 2, 3)[g], ("hT", 0, g)
    for g in range(KD // 2):
        yield 4 + g, ("hT", 1, g)
    for half in range(2):
        for c in range(UF // 2):
            for f in range(2):
                yield f, ("up", half, c, f)
        for d in range(2):
            for t in range(TILES):
                yield 2 + t, ("down", half, d, t)
    for k in range(KD):
        yield 6 + k % 2, ("xT", k)


def attention_uses(i):
    for p in range(2):
        yield 2 + p, ("score", i - C_Q, p)
    if i > C_Q:
        for p in range(2):
            yield 6 + p, ("pT", i - C_Q - 1, p)


def levels_of(hs):
    return 2 * (hs % 4), 2 * (hs % 4) + 1


def state_uses(what, c):
    last = c == TILES - 1
    if what == "kT":
        yield 0 if last else 2, ("kT", c)
    elif what == "su":
        for p in range(2):
            yield (6 + p if last else 3 - p), ("su", c, p)
    elif what == "o":
        for p in range(2):
            yield (6 + p if last else 4 + p), ("o", c, p)
    else:
        yield c[0] % 2, ("oT",) + c


STATE_STEPS = {8: [("kT", 0)], 9: [("su", 0), ("o", 0)], 10: [("kT", 1)], 11: [("su", 1), ("o", 1)],
               12: [("kT", 2)], 13: [("su", 2), ("o", 2)]}

EARLY = UseOrder(early_uses())
USES = UseOrder(block_uses())


def build(nc, x, mem, norm_mix, norm_mem, w_kv, w_out, norm_mlp, w_up, w_down, w_in, w_gate2, b_gate,
          out_gain, final_norm, level_masks, identity, scan_mask, out):
    with ExitStack() as ctx:
        def sb(name, shape, dt=F32):
            return ctx.enter_context(nc.sbuf_tensor(name, shape, dt))

        def sem(name):
            return ctx.enter_context(nc.semaphore(name))

        h_hi = sb("h_hi", [P, KD, BLOCK], F32R)
        h_lo = sb("h_lo", [P, KD, BLOCK], F32R)
        raw = sb("raw", [P, 2, CHUNK])
        w_hi = sb("w_hi", [P, 2, CHUNK], F32R)
        w_lo = sb("w_lo", [P, 2, CHUNK], F32R)
        kmT = sb("kmT", [P, XH, MEM])
        vm = sb("vm", [P, MT, XD])
        carried_state = sb("carried_state", [P, HEADS, DV])
        scratch = sb("scratch", [P, 2, BLOCK])
        keys = sb("keys", [P, 2, HEADS, P])
        gain_fin = sb("gain_fin", [P, D])
        w2 = sb("w2", [RANK, HEADS * DK])
        ident = sb("ident", [P, P])
        masks = sb("masks", [P, len(WIDTHS), HALF], U8)
        scanm = sb("scanm", [P, BLOCK], U8)
        wg_hi = sb("wg_hi", [P, KD, RANK], F32R)
        wg_lo = sb("wg_lo", [P, KD, RANK], F32R)
        gain_mem = sb("gain_mem", [P, KD])
        gain_mix = sb("gain_mix", [P, KD])
        gain_mlp = sb("gain_mlp", [P, KD])
        gate_bias = sb("gate_bias", [P, HEADS])
        gain_o = sb("gain_o", [P, DV // P])
        half_gain_o = sb("half_gain_o", [P, DV // P])
        minus_half = sb("minus_half", [P, HEADS])
        ssq = sb("ssq", [P, 3, TILES])
        ms = sb("ms", [P, 3, TILES])
        rstd = sb("rstd", [P, 3, TILES])
        o_ssq = sb("o_ssq", [P, TILES, HEADS])
        o_ms = sb("o_ms", [P, TILES, HEADS])
        o_rstd = sb("o_rstd", [P, TILES, HEADS])
        chunk_decay = sb("chunk_decay", [P, TILES, HEADS])
        top = sb("top", [P, TILES, XH])
        neg_top = sb("neg_top", [P, TILES, XH])
        den = sb("den", [P, TILES, XH])
        rden = sb("rden", [P, TILES, XH])

        with ExitStack() as mixers:
            def mx(name, shape, dt=F32):
                return mixers.enter_context(nc.sbuf_tensor(name, shape, dt))

            q = mx("q", [P, HEADS, BLOCK])
            k_ = mx("k", [P, HEADS, BLOCK])
            b_ = mx("b", [P, HEADS, BLOCK])
            xq_a = mx("xq_a", [P, TILES, BLOCK])
            v = mx("v", [P, TILES, D])
            dec = mx("dec", [P, 2, HEADS, P])
            queries = mx("queries", [P, 2, HEADS, HALF])
            y_rows = mx("y_rows", [P, 2, BLOCK])
            inner_state = mx("inner_state", [P, HEADS, DV])
            o_junk = mx("o_junk", [P, HEADS, DV], BF16)
            sr = mx("sr", [P, KD, BLOCK])
            mem_hi = mx("mem_hi", [P, XH, BLOCK], F32R)
            mem_lo = mx("mem_lo", [P, XH, BLOCK], F32R)
        with ExitStack() as mlp:
            u_hi = mlp.enter_context(nc.sbuf_tensor("u_hi", [P, UF, BLOCK], F32R))
            u_lo = mlp.enter_context(nc.sbuf_tensor("u_lo", [P, UF, BLOCK], F32R))
            xres = mlp.enter_context(nc.sbuf_tensor("xres", [P, TILES, D], F32))
            xin = mlp.enter_context(nc.sbuf_tensor("xin", [P, TILES, D], F32))
        with ExitStack() as norm:
            hn = norm.enter_context(nc.sbuf_tensor("hn", [P, TILES, D], F32))
        states = [carried_state, inner_state]
        probs, probsT = v[:, 0:2, :], v[:, 2:4, :]
        gT = dec[0:RANK, 0].rearrange("p h t -> p (h t)")
        soft = sr[:, 0:HEADS, :]
        o_n = [v[:, c, :] for c in range(TILES - 1)] + [q[:].rearrange("p h t -> p (h t)")[:, 0:D]]
        masks_raw = dec[:].rearrange("p a h t -> p (a h t)")[:, 0:len(WIDTHS) * HALF]
        scan_raw = scratch[:, 1, :]
        wg_raw = scratch[:, 0, 0:KD * RANK].rearrange("p (k c) -> p k c", k=KD)

        banks = ctx.enter_context(nc.psum_tensor("banks", [P, 8, 512], F32))

        bank_full = [sem(f"bank_full{b}") for b in range(8)]
        bank_read = [sem(f"bank_read{b}") for b in range(8)]
        raw_loaded = [Signal(sem(f"raw_loaded{s}"), KV_CHUNKS // 2, CHUNKS // 2, 16) for s in range(2)]
        hi_split = Signal(sem("hi_split"), KV_CHUNKS, CHUNKS)
        lo_split = Signal(sem("lo_split"), KV_CHUNKS, CHUNKS)
        weights_used = Signal(sem("weights_used"), KV_CHUNKS, CHUNKS)
        first_consts_loaded = sem("first_consts_loaded")
        consts_loaded = sem("consts_loaded")
        mem_loaded = sem("mem_loaded")
        xin_loaded = Signal(sem("xin_loaded"), 1, 1, 16)
        xres_loaded = Signal(sem("xres_loaded"), 0, 1, 16)
        out_stored = Signal(sem("out_stored"), 1, TILES, 16)
        ssq_ready = Signal(sem("ssq_ready"), MT + TILES, 3 * TILES)
        ms_ready = Signal(sem("ms_ready"), MT + TILES, 3 * TILES)
        rstd_ready = Signal(sem("rstd_ready"), MT + TILES, 3 * TILES)
        normed = Signal(sem("normed"), MT + TILES, 2 * TILES)
        hi_part = Signal(sem("hi_part"), 2 * KD, 2 * TILES + 2 * KD)
        minus_half_set = sem("minus_half_set")
        keys_set = sem("keys_set")
        wg_hi_ready = sem("wg_hi_ready")
        wg_ready = sem("wg_ready")
        half_gain_ready = sem("half_gain_ready")
        soft_ready = Signal(sem("soft_ready"), 0, HEADS)
        soft_exp = Signal(sem("soft_exp"), 0, 1)
        b_ready = Signal(sem("b_ready"), 0, 1)
        top_ready = Signal(sem("top_ready"), 0, 2 * TILES)
        probs_ready = Signal(sem("probs_ready"), 0, 2 * TILES)
        gap_ready = Signal(sem("gap_ready"), 0, TILES * (DECAYS - 1))
        decay_ready = Signal(sem("decay_ready"), 0, TILES * DECAYS)
        product_ready = Signal(sem("product_ready"), 0, TILES * DECAYS)
        chunk_decay_ready = Signal(sem("chunk_decay_ready"), 0, TILES)
        gate_tanh_ready = Signal(sem("gate_tanh_ready"), 0, KD)
        o_ssq_ready = Signal(sem("o_ssq_ready"), 0, TILES)
        o_ms_ready = Signal(sem("o_ms_ready"), 0, TILES)
        o_rstd_ready = Signal(sem("o_rstd_ready"), 0, TILES)
        y_hi_ready = Signal(sem("y_hi_ready"), 0, 2 * TILES)
        mix_ready = Signal(sem("mix_ready"), 0, 2 * TILES)
        square_ready = Signal(sem("square_ready"), 0, 2 * UF)
        u_ready = Signal(sem("u_ready"), 2, 2 * UF)
        out_ready = Signal(sem("out_ready"), 0, TILES)
        dve_step = sem("dve_step")

        def full(n, name, more=0):
            bank, index = USES.place[name]
            return bank_full[bank], n * USES.count[bank] + more + (EARLY.count[bank] + index + 1)

        def empty(n, name, more=0):
            bank, index = USES.place[name]
            return bank_read[bank], n * USES.count[bank] + more + (EARLY.count[bank] + index)

        def read(n, name, more=0):
            bank, index = USES.place[name]
            return bank_read[bank], n * USES.count[bank] + more + (EARLY.count[bank] + index + 1)

        def early_full(name):
            bank, index = EARLY.place[name]
            return bank_full[bank], index + 1

        def early_empty(name):
            bank, index = EARLY.place[name]
            return bank_read[bank], index

        def early_read(name):
            bank, index = EARLY.place[name]
            return bank_read[bank], index + 1

        def bank_of(name):
            return (USES.place if name in USES.place else EARLY.place)[name][0]

        def bank(name):
            return banks[:, bank_of(name), :]

        def heads_of(ap, heads=HEADS):
            return ap.rearrange("p (h t) -> p h t", h=heads)

        def at_chunk(tensor, c):
            return tensor[:, :, c * P:(c + 1) * P]

        def spans(ap, w, upper):
            return ap.rearrange("p h (s a w) -> p h s a w", a=2, w=w)[:, :, :, int(upper), :]

        def packed(ap, w):
            return ap.rearrange("p h (s w) -> p h s w", w=w)

        def rows(w):
            return w.rearrange("(k p) c -> p k c", p=P)

        win, wout, wup, wdown, wkv = rows(w_in), rows(w_out), rows(w_up), rows(w_down), rows(w_kv)
        x_tiles = x.rearrange("(t p) d -> p t d", p=P)
        out_tiles = out.rearrange("(t p) d -> p t d", p=P)
        mem_tiles = mem.rearrange("(t p) d -> p t d", p=P)
        first_cols = {C_XQ: COL_XQ, C_Q: COL_Q, C_K: COL_K, C_R: COL_R}

        def y_row(c):
            return scratch[:, c, :] if c < 2 else y_rows[:, c - 2, :]

        def chunk_source(i):
            i %= CHUNKS
            if i >= C_OUT:
                d, kg = (i - C_OUT) // 3, OUT_ORDER[(i - C_OUT) % 3]
                return wout[:, KG * kg:KG * (kg + 1), 512 * d:512 * (d + 1)]
            if C_V <= i < C_R:
                d, kg = divmod(i - C_V, 2)
                return win[:, KG * kg:KG * (kg + 1), COL_V + 512 * d:COL_V + 512 * (d + 1)]
            start = max(s for s in first_cols if s <= i)
            col = first_cols[start] + FCOLS * (i - start)
            return win[:, :, col:col + FCOLS]

        def as_kblocks(tensor, slot, kblocks):
            return tensor[:, slot, :].rearrange("p (k c) -> p k c", k=kblocks)

        block = ctx.enter_context(nc.Block())

        @block.sync
        def _(sp):
            def load(n, i, slot, source, kblocks):
                sp.wait_ge(*hi_split.at(n, i - 2))
                sp.wait_ge(*lo_split.at(n, i - 2))
                sp.dma_start(as_kblocks(raw, slot, kblocks), source).then_inc(raw_loaded[slot].sem, 16)

            sp.dma_start(xres[:, 0:MT, :], mem_tiles).then_inc(mem_loaded, 16)
            for i in range(KV_CHUNKS):
                if i >= 2:
                    sp.wait_ge(*hi_split.early(i - 2))
                    sp.wait_ge(*lo_split.early(i - 2))
                sp.dma_start(as_kblocks(raw, i % 2, KD), wkv[:, :, FCOLS * i:FCOLS * (i + 1)])\
                    .then_inc(raw_loaded[i % 2].sem, 16)
                if i == 1:
                    sp.dma_start(xin[:, :, :], x_tiles[:, 0:TILES, :]).then_inc(xin_loaded.sem, 16)
            load(0, 0, 0, chunk_source(0), KD)
            with sp.Fori(0, BLOCKS) as n:
                x_row = sp.snap(n * TILES)
                x_next = sp.snap(((n + 1) % BLOCKS) * TILES)
                for i in range(1, C_UP[0]):
                    load(n, i, i % 2, chunk_source(i), KD if i < C_V or C_R <= i < C_OUT else KG)
                    if i == C_OUT + 3:
                        sp.wait_ge(*read(n, ("oT", TILES - 1, 1)))
                        sp.dma_start(xres[:, :, :], x_tiles[:, bass.ds(x_row, TILES), :])\
                            .then_inc(xres_loaded.sem, 16)
                for half in range(2):
                    with sp.Fori(0, UF // 4) as j:
                        for c in range(2):
                            col = sp.snap(j * (2 * FCOLS) + (half * HALF_HIDDEN + c * FCOLS))
                            load(n, j * 2 + (C_UP[half] + c), c, wup[:, :, bass.ds(col, FCOLS)], KD)
                    if half == 0:
                        sp.wait_ge(*weights_used.at(n, C_UP[0] - 1))
                        sp.dma_start(xin[:, :, :], x_tiles[:, bass.ds(x_next, TILES), :])\
                            .then_inc(xin_loaded.sem, 16)
                    with sp.Fori(0, 2) as d:
                        col = sp.snap(d * 512)
                        for kg in range(UF // KG):
                            k0 = half * UF + KG * kg
                            load(n, d * 4 + (C_DOWN[half] + kg), kg % 2,
                                 wdown[:, k0:k0 + KG, bass.ds(col, 512)], KG)
                load(n, CHUNKS, 0, chunk_source(0), KD)

        @block.gpsimd
        def _(pool):
            nc.gpsimd.memset(minus_half[:], -0.5).then_inc(minus_half_set, 1)
            nc.gpsimd.memset(keys[:], 0.0).then_inc(keys_set, 1)
            for tile, source in [(wg_raw, win[:, :, COL_G:COL_G + RANK]), (scan_raw, scan_mask), (masks_raw, level_masks),
                                 (gain_o[:], out_gain), (w2[:], w_gate2), (gate_bias[:], b_gate), (gain_mlp[:], norm_mlp),
                                 (gain_fin[:], final_norm.rearrange("(a d) -> a d", a=1).broadcast_to([P, D]))]:
                pool.dma_start(tile, source).then_inc(consts_loaded, 16)
            pool.wait_ge(minus_half_set, 1)

            def rsqrt(n, which, t):
                e = which * TILES + t
                pool.wait_ge(*ms_ready.at(n, e))
                nc.gpsimd.tensor_tensor(rstd[:, which, t:t + 1], ms[:, which, t:t + 1], minus_half[:, 0:1],
                                        ALU.pow).then_inc(rstd_ready.sem, 1)

            for e in range(MT + TILES):
                which, t = (0, e) if e < MT else (1, e - MT)
                pool.wait_ge(*ms_ready.early(e))
                nc.gpsimd.tensor_tensor(rstd[:, which, t:t + 1], ms[:, which, t:t + 1], minus_half[:, 0:1],
                                        ALU.pow).then_inc(rstd_ready.sem, 1)
            pool.wait_ge(keys_set, 1)

            def level_product(n, c, level):
                e, w = c * DECAYS + level - 1, WIDTHS[level - 1]
                slot = e % 2
                pool.wait_ge(*decay_ready.at(n, e))
                if level >= 3:
                    pool.wait_ge(*full(n, ("level", c, level - 2)))
                elif c:
                    pool.wait_ge(*full(n, ("level", c - 1, LEVELS - 1)))
                ring = level % 2
                if w > 1:
                    nc.gpsimd.tensor_tensor(spans(keys[:, ring], w, False), spans(at_chunk(k_, c), w, False),
                                            spans(dec[:, slot], w, False), ALU.mult)
                nc.gpsimd.tensor_tensor(packed(queries[:, ring], w), spans(at_chunk(q, c), w, True),
                                        spans(dec[:, slot], w, True), ALU.mult).then_inc(product_ready.sem, 1)

            def end_products(n, c):
                pool.wait_ge(*full(n, ("level", c, LEVELS - 1)))
                for e, tensor in ((QUERY_DECAY, q), (KEY_DECAY, k_)):
                    pool.wait_ge(*decay_ready.at(n, c * DECAYS + e))
                    nc.gpsimd.tensor_tensor(at_chunk(tensor, c), at_chunk(tensor, c),
                                            dec[:, (c * DECAYS + e) % 2], ALU.mult).then_inc(product_ready.sem, 1)

            with pool.Fori(0, BLOCKS) as n:
                for f in range(2):
                    pool.wait_ge(*read(n, ("k", 2 + f)))
                def o_rsqrt(c):
                    pool.wait_ge(*o_ms_ready.at(n, c))
                    nc.gpsimd.tensor_tensor(o_rstd[:, c, :], o_ms[:, c, :], minus_half[:], ALU.pow)\
                        .then_inc(o_rstd_ready.sem, 1)

                def y_low(c, p):
                    pool.wait_ge(*y_hi_ready.at(n, p * TILES + c))
                    hi = at_chunk(h_hi[:, 4 * p:4 * p + 4, :].bitcast(F32), c)
                    nc.gpsimd.tensor_tensor(at_chunk(h_lo[:, 4 * p:4 * p + 4, :], c), heads_of(y_row(c)), hi,
                                            ALU.subtract).then_inc(mix_ready.sem, 1)

                for hs in range(STEPS):
                    c = hs // 4
                    if hs % 4 == 0 and c:
                        end_products(n, c - 1)
                    for level in levels_of(hs):
                        if level:
                            level_product(n, c, level)
                    if hs in (10, 12, 14):
                        o_rsqrt(hs // 2 - 5)
                end_products(n, TILES - 1)
                o_rsqrt(TILES - 1)
                for p in range(2):
                    for c in range(TILES):
                        y_low(c, p)
                for which in range(3):
                    for t in range(TILES):
                        rsqrt(n, which, t)

        @block.scalar
        def _(act):
            def split_hi(n, i, slot, pair):
                act.wait_ge(*raw_loaded[slot].at(n, pair))
                act.wait_ge(*weights_used.at(n, i - 2))
                nc.scalar.activation(w_hi[:, slot, :], raw[:, slot, :], ACT.Copy).then_inc(hi_split.sem, 1)

            def square(which, t, source):
                nc.scalar.activation(hn[:, t, :], source[:, t, :], ACT.Square, accum_out=ssq[:, which, t:t + 1])\
                    .then_inc(ssq_ready.sem, 1)

            for tile, source in [(ident, identity), (gain_mem, norm_mem), (gain_mix, norm_mix)]:
                act.dma_start(tile[:], source).then_inc(first_consts_loaded, 16)
            act.wait_ge(mem_loaded, 16)
            for t in range(MT):
                square(0, t, xres)

            def first_split_hi(i):
                act.wait_ge(*raw_loaded[i].early(0))
                nc.scalar.activation(w_hi[:, i, :], raw[:, i, :], ACT.Copy).then_inc(hi_split.sem, 1)

            first_split_hi(0)
            act.wait_ge(first_consts_loaded, 16 * 3)
            for k in range(KD):
                act.wait_ge(*early_full(("memT", k)))
                nc.scalar.activation(h_hi[:, k, 0:MEM], bank(("memT", k))[:, 0:MEM], ACT.Copy,
                                     scale=gain_mem[:, k:k + 1]).then_inc(hi_part.sem, 1)
            first_split_hi(1)
            act.wait_ge(*xin_loaded.early(0))
            for t in range(TILES):
                act.wait_ge(*normed.early(MT - 1))
                square(1, t, xin)
            for i in range(KV_CHUNKS):
                if i < 2:
                    for f in range(2):
                        h = 2 * i + f
                        act.wait_ge(*early_full(("km", h)))
                        nc.scalar.activation(kmT[:, h, :], bank(("km", h))[:, 0:MEM], ACT.Copy)\
                            .then_inc(bank_read[bank_of(("km", h))], 1)
                if i + 2 <= KV_CHUNKS:
                    act.wait_ge(*raw_loaded[i % 2].early((i + 2) // 2))
                    act.wait_ge(*weights_used.early(i))
                    nc.scalar.activation(w_hi[:, i % 2, :], raw[:, i % 2, :], ACT.Copy).then_inc(hi_split.sem, 1)
            act.wait_ge(consts_loaded, 16 * 8)
            nc.scalar.activation(wg_hi[:], wg_raw, ACT.Copy).then_inc(wg_hi_ready, 1)
            for k in range(KD):
                act.wait_ge(*early_full(("x0T", k)))
                nc.scalar.activation(h_hi[:, k, :], bank(("x0T", k)), ACT.Copy,
                                     scale=gain_mix[:, k:k + 1]).then_inc(hi_part.sem, 1)

            with act.Fori(0, BLOCKS) as n:
                def next_chunk(i):
                    split_hi(n, i + 1, (i + 1) % 2, (i + 1) // 2)

                def copy_out(name, to, scale=1.0):
                    act.wait_ge(*full(n, name))
                    nc.scalar.activation(to, bank(name), ACT.Copy, scale=scale)\
                        .then_inc(bank_read[bank_of(name)], 1)

                def attention_exp(t):
                    for p in range(2):
                        act.wait_ge(*top_ready.at(n, 2 * t + p))
                        for h in (2 * p, 2 * p + 1):
                            last = nc.scalar.activation(
                                probs[:, t % 2, h * MEM:(h + 1) * MEM],
                                bank(("score", t, p))[:, (h % 2) * MEM:(h % 2 + 1) * MEM], ACT.Exp,
                                bias=neg_top[:, t, h:h + 1], scale=XSCALE, accum_out=den[:, t, h:h + 1])
                        last.then_inc(bank_read[bank_of(("score", t, p))], 1)

                def attention_probsT(t):
                    for p in range(2):
                        copy_out(("pT", t, p), probsT[:, t % 2, p * 512:(p + 1) * 512])

                def attention_hi(t):
                    for p in range(2):
                        act.wait_ge(*full(n, ("pv", t, p)))
                        nc.scalar.activation(at_chunk(mem_hi[:, 2 * p:2 * p + 2, :], t),
                                             heads_of(bank(("pv", t, p))[:, 0:2 * P], 2), ACT.Copy)\
                            .then_inc(hi_part.sem, 1)

                def decay(c, e):
                    if e != QUERY_DECAY:
                        act.wait_ge(*gap_ready.at(n, c * (DECAYS - 1) + min(e, DECAYS - 2)))
                        source = dec[:, (c * DECAYS + e) % 2]
                    else:
                        act.wait_ge(*b_ready.at(n, 0))
                        act.wait_ge(*product_ready.at(n, c * DECAYS + e - 2))
                        source = at_chunk(b_, c)
                    nc.scalar.activation(dec[:, (c * DECAYS + e) % 2], source, ACT.Exp, scale=1.0 / TAU)\
                        .then_inc(decay_ready.sem, 1)

                def end_decays(c):
                    decay(c, QUERY_DECAY)
                    decay(c, KEY_DECAY)
                    nc.scalar.activation(chunk_decay[:, c, :], b_[:, :, (c + 1) * P - 1], ACT.Exp, scale=1.0 / TAU)\
                        .then_inc(chunk_decay_ready.sem, 1)

                next_chunk(0)
                for f in range(2):
                    copy_out(("xq", f), xq_a[:, f, :])
                next_chunk(1)
                for f in range(2, 4):
                    copy_out(("xq", f), xq_a[:, f, :])
                act.wait_ge(*out_stored.at(n, -1))
                for h in range(HEADS):
                    act.wait_ge(*full(n, ("z", h)))
                    nc.scalar.activation(b_[:, h, :], bank(("z", h)), ACT.Identity, bias=gate_bias[:, h:h + 1])
                    nc.scalar.activation(soft[:, h, :], bank(("z", h)), ACT.Abs, bias=gate_bias[:, h:h + 1])\
                        .then_inc(bank_read[bank_of(("z", h))], 1)
                next_chunk(C_Q)
                for h in range(HEADS):
                    act.wait_ge(*read(n, ("z", h)))
                    last = nc.scalar.activation(soft[:, h, :], soft[:, h, :], ACT.Exp, scale=-1.0)
                last.then_inc(soft_exp.sem, 1)
                for f in range(2):
                    copy_out(("q", f), q[:, f, :], QSCALE)
                act.wait_ge(*soft_exp.at(n, 0))
                for h in range(HEADS):
                    nc.scalar.activation(soft[:, h, :], soft[:, h, :], ACT.Ln, bias=1.0).then_inc(soft_ready.sem, 1)
                attention_exp(0)
                for i in range(C_Q + 1, C_V):
                    next_chunk(i)
                    if i < C_K:
                        copy_out(("q", 2), q[:, 2, :], QSCALE)
                    if i - C_K >= 0:
                        attention_hi(i - C_K)
                    if i < C_K:
                        copy_out(("q", 3), q[:, 3, :], QSCALE)
                    attention_exp(i - C_Q)
                    attention_probsT(i - C_Q - 1)

                def o_square(c):
                    for h in range(HEADS):
                        act.wait_ge(*full(n, ("o", c, h // 2)))
                        last = nc.scalar.activation(
                            o_junk[:, h, :], bank(("o", c, h // 2))[:, (h % 2) * DV:(h % 2 + 1) * DV], ACT.Square,
                            accum_out=o_ssq[:, c, h:h + 1])
                    last.then_inc(o_ssq_ready.sem, 1)

                def o_norm(c):
                    act.wait_ge(*o_rstd_ready.at(n, c))
                    for h in range(HEADS):
                        ins = nc.scalar.activation(
                            o_n[c][:, h * DV:(h + 1) * DV],
                            bank(("o", c, h // 2))[:, (h % 2) * DV:(h % 2 + 1) * DV], ACT.Copy,
                            scale=o_rstd[:, c, h:h + 1])
                        if h % 2:
                            ins.then_inc(bank_read[bank_of(("o", c, h // 2))], 1)

                def keys_back(c):
                    act.wait_ge(*full(n, ("kT", c)))
                    nc.scalar.activation(at_chunk(k_, c), heads_of(bank(("kT", c))), ACT.Copy)\
                        .then_inc(bank_read[bank_of(("kT", c))], 1)

                def y_high(c, p):
                    act.wait_ge(*read(n, ("oT", c, p)))
                    nc.scalar.activation(at_chunk(h_hi[:, 4 * p:4 * p + 4, :], c), heads_of(y_row(c)), ACT.Copy)\
                        .then_inc(y_hi_ready.sem, 1)

                def gate_tanh(f):
                    act.wait_ge(*empty(n, ("r", f)))
                    act.wait_ge(*full(n, ("r", f)))
                    nc.scalar.activation(scratch[:, f % 2, :], bank(("r", f)), ACT.Tanh, scale=0.5)\
                        .then_inc(gate_tanh_ready.sem, 1)

                decay(0, 0)
                for hs in range(STEPS):
                    i, c = C_V + hs // 2, hs // 4
                    if hs % 4 == 0 and c:
                        decay(c, 0)
                    if hs in (9, 11, 13):
                        keys_back(hs // 2 - 4)
                    if hs in (11, 13, 15):
                        o_norm(hs // 2 - 5)
                    if hs % 2 == 0:
                        next_chunk(i)
                    if hs == 0:
                        attention_probsT(TILES - 1)
                    if hs in (1, 3):
                        attention_hi(2 + hs // 2)
                    before = hs - 1
                    if 0 <= before < 8 and before // 2 % 2 == 1:
                        d = before // 4
                        for t in (2 * (before % 2), 2 * (before % 2) + 1):
                            copy_out(("v", d, t), v[:, t, 512 * d:512 * (d + 1)])
                    if hs in (10, 12, 14):
                        o_square(hs // 2 - 5)
                    if hs >= 9:
                        gate_tanh(hs - 9)
                    if hs % 4 == 3:
                        end_decays(c)
                    else:
                        for level in levels_of(hs + 1):
                            decay(c, level - 1)

                gate_tanh(KD - 1)
                next_chunk(C_OUT)
                o_square(TILES - 1)
                keys_back(TILES - 1)
                for c in range(TILES - 1):
                    if c == 1:
                        o_norm(TILES - 1)
                    y_high(c, 0)
                y_high(TILES - 1, 0)
                next_chunk(C_OUT + 1)
                for c in range(TILES):
                    y_high(c, 1)

                def h_high(h, g):
                    act.wait_ge(*full(n, ("hT", h, g)))
                    for j in range(2):
                        last = nc.scalar.activation(h_hi[:, 2 * g + j, h * 256:(h + 1) * 256],
                                                    bank(("hT", h, g))[:, j * 256:(j + 1) * 256], ACT.Copy,
                                                    scale=gain_mlp[:, 2 * g + j:2 * g + j + 1])
                    last.then_inc(hi_part.sem, 1)

                for i in range(C_OUT + 2, C_UP[0]):
                    next_chunk(i)
                for t in range(TILES):
                    if t == TILES - 1:
                        h_high(0, 0)
                        h_high(0, 1)
                    act.wait_ge(*read(n, ("out", 1, t)))
                    square(0, t, xres)
                for h, g in [(0, 2), (0, 3), (1, 0), (1, 1), (1, 2), (1, 3)]:
                    h_high(h, g)

                for half in range(2):
                    with act.Fori(0, UF // 4) as j:
                        for c in range(2):
                            i = C_UP[half] + c
                            split_hi(n, j * 2 + (i + 1), (i + 1) % 2, j + (i + 1) // 2)
                            for f in range(2):
                                e = j * 4 + (half * UF + 2 * c + f)
                                act.wait_ge(*full(n, ("up", half, c, f), j * 2))
                                act.wait_ge(*u_ready.at(n, e - 2))
                                nc.scalar.activation(scratch[:, f, :], banks[:, f, :], ACT.Relu)\
                                    .then_inc(bank_read[f], 1)
                                act.wait_ge(*read(n, ("up", half, c, f), j * 2))
                                nc.scalar.activation(scratch[:, f, :], scratch[:, f, :], ACT.Square)\
                                    .then_inc(square_ready.sem, 1)
                    with act.Fori(0, 2) as d:
                        for kg in range(UF // KG):
                            i = C_DOWN[half] + kg
                            split_hi(n, d * 4 + (i + 1), (i + 1) % 2, d * 2 + (i + 1) // 2)
                            if half == 1:
                                act.wait_ge(*full(n, ("xT", kg), d * 2))
                                nc.scalar.activation(h_hi[:, bass.ds(d * 4 + kg, 1), :],
                                                     banks[:, 6 + kg % 2:7 + kg % 2, :], ACT.Copy,
                                                     scale=gain_mix[:, bass.ds(d * 4 + kg, 1)])\
                                    .then_inc(hi_part.sem, 1)
                    if half == 0:
                        act.wait_ge(*xin_loaded.at(n, 0))
                        act.wait_ge(*full(n, ("down", 0, 1, TILES - 1)))
                        for t in range(TILES):
                            square(1, t, xin)
                for t in range(TILES):
                    act.wait_ge(*read(n, ("down", 1, 1, t)))
                    square(2, t, xres)
                out_tile = act.snap(n * TILES)
                for t in range(TILES):
                    act.wait_ge(*out_ready.at(n, t))
                    act.dma_start(out_tiles[:, bass.ds(out_tile + t, 1), :], xres[:, t:t + 1, :])\
                        .then_inc(out_stored.sem, 16)
            act.wait_ge(*out_stored.at(BLOCKS - 1, TILES - 1))

        @block.vector
        def _(dve):
            steps = [0]

            def link(ins):
                steps[0] += 1
                ins.then_inc(dve_step, 1)
                dve.wait_ge(dve_step, steps[0])

            def restart():
                dve.sem_clear(dve_step)
                steps[0] = 0

            def split_lo(n, i, slot):
                dve.wait_ge(*hi_split.at(n, i))
                nc.vector.tensor_tensor(w_lo[:, slot, :], raw[:, slot, :], w_hi[:, slot, :].bitcast(F32),
                                        ALU.subtract).then_inc(lo_split.sem, 1)

            def mean_square(which, t):
                nc.vector.tensor_scalar(ms[:, which, t:t + 1], ssq[:, which, t:t + 1], 1.0 / D, EPS,
                                        ALU.mult, ALU.add).then_inc(ms_ready.sem, 1)

            def scale_tile(which, t, source, to):
                nc.vector.tensor_scalar(to[:, t, :], source[:, t, :], rstd[:, which, t:t + 1], None,
                                        ALU.mult).then_inc(normed.sem, 1)

            def low(name, k, gain, cols=BLOCK):
                nc.vector.scalar_tensor_tensor(
                    out=h_lo[:, k, 0:cols], in0=bank((name, k))[:, 0:cols], scalar=gain[:, k:k + 1],
                    in1=h_hi[:, k, 0:cols].bitcast(F32), op0=ALU.mult, op1=ALU.subtract)\
                    .then_inc(bank_read[bank_of((name, k))], 1)

            nc.vector.memset(carried_state[:], 0.0).then_inc(u_ready.sem, 2)
            nc.vector.nop().then_inc(out_stored.sem, 16)
            for t in range(MT):
                dve.wait_ge(*ssq_ready.early(t))
                mean_square(0, t)
            for t in range(MT):
                dve.wait_ge(*rstd_ready.early(t))
                scale_tile(0, t, xres, xres)

            def first_split_lo(i):
                dve.wait_ge(*hi_split.early(i))
                nc.vector.tensor_tensor(w_lo[:, i, :], raw[:, i, :], w_hi[:, i, :].bitcast(F32),
                                        ALU.subtract).then_inc(lo_split.sem, 1)

            first_split_lo(0)
            dve.wait_ge(first_consts_loaded, 16 * 3)
            for k in range(KD):
                dve.wait_ge(*hi_part.early(k))
                low("memT", k, gain_mem, MEM)
            first_split_lo(1)
            for t in range(TILES):
                dve.wait_ge(*ssq_ready.early(MT + t))
                mean_square(1, t)
            for t in range(TILES):
                dve.wait_ge(*rstd_ready.early(MT + t))
                scale_tile(1, t, xin, xin)
            for i in range(KV_CHUNKS):
                if i >= 2:
                    for m in range(MT):
                        name = ("vm", i - 2, m)
                        dve.wait_ge(*early_full(name))
                        nc.vector.tensor_copy(vm[:, m, (i - 2) * FCOLS:(i - 1) * FCOLS], bank(name)[:, 0:FCOLS])\
                            .then_inc(bank_read[bank_of(name)], 1)
                if i + 2 <= KV_CHUNKS:
                    dve.wait_ge(*hi_split.early(i + 2))
                    nc.vector.tensor_tensor(w_lo[:, i % 2, :], raw[:, i % 2, :], w_hi[:, i % 2, :].bitcast(F32),
                                            ALU.subtract).then_inc(lo_split.sem, 1)
            dve.wait_ge(consts_loaded, 16 * 8)
            nc.vector.tensor_copy(masks[:].rearrange("p l t -> p (l t)"), masks_raw)
            nc.vector.tensor_copy(scanm[:], scan_raw)
            nc.vector.tensor_scalar(half_gain_o[:], gain_o[:], 0.5, None, ALU.mult).then_inc(half_gain_ready, 1)
            dve.wait_ge(wg_hi_ready, 1)
            nc.vector.tensor_tensor(wg_lo[:], wg_raw, wg_hi[:].bitcast(F32), ALU.subtract).then_inc(wg_ready, 1)
            for k in range(KD):
                dve.wait_ge(*hi_part.early(KD + k))
                low("x0T", k, gain_mix)

            dve.wait_ge(half_gain_ready, 1)
            with dve.Fori(0, BLOCKS) as n:
                def next_chunk(i):
                    split_lo(n, i + 1, (i + 1) % 2)

                def attention_top(t):
                    for p in range(2):
                        dve.wait_ge(*full(n, ("score", t, p)))
                        link(nc.vector.reduce_max(top[:, t, 2 * p:2 * p + 2],
                                                  heads_of(bank(("score", t, p)), 2), AX_X))
                        nc.vector.tensor_scalar(neg_top[:, t, 2 * p:2 * p + 2], top[:, t, 2 * p:2 * p + 2],
                                                -XSCALE, None, ALU.mult).then_inc(top_ready.sem, 1)

                def attention_norm(t):
                    for p in range(2):
                        dve.wait_ge(*read(n, ("score", t, p)))
                        link(nc.vector.reciprocal(rden[:, t, 2 * p:2 * p + 2], den[:, t, 2 * p:2 * p + 2]))
                        for h in (2 * p, 2 * p + 1):
                            row = probs[:, t % 2, h * MEM:(h + 1) * MEM]
                            last = nc.vector.tensor_scalar(row, row, rden[:, t, h:h + 1], None, ALU.mult)
                        last.then_inc(probs_ready.sem, 1)

                def attention_low(t):
                    for p in range(2):
                        dve.wait_ge(*hi_part.at(n, 2 * t + p))
                        nc.vector.tensor_tensor(
                            at_chunk(mem_lo[:, 2 * p:2 * p + 2, :], t), heads_of(bank(("pv", t, p))[:, 0:2 * P], 2),
                            at_chunk(mem_hi[:, 2 * p:2 * p + 2, :].bitcast(F32), t), ALU.subtract)\
                            .then_inc(bank_read[bank_of(("pv", t, p))], 1)

                def copy_k(f):
                    dve.wait_ge(*full(n, ("k", f)))
                    nc.vector.tensor_copy(k_[:, f, :], bank(("k", f))).then_inc(bank_read[bank_of(("k", f))], 1)

                def level_gap(c, level):
                    e, w = c * DECAYS + level - 1, WIDTHS[level - 1]
                    slot, b = e % 2, at_chunk(b_, c)
                    if e >= 2:
                        dve.wait_ge(*product_ready.at(n, e - 2))
                    lower, upper = spans(b, w, False), spans(b, w, True)
                    last_lower = lower[:, :, :, w - 1:w].broadcast_to([P, HEADS, HALF // w, w])
                    if w > 1:
                        nc.vector.tensor_tensor(spans(dec[:, slot], w, False), last_lower, lower, ALU.subtract)
                    nc.vector.tensor_tensor(spans(dec[:, slot], w, True), upper, last_lower, ALU.subtract)\
                        .then_inc(gap_ready.sem, 1)

                def end_gap(c):
                    e, b = c * DECAYS + KEY_DECAY, at_chunk(b_, c)
                    dve.wait_ge(*product_ready.at(n, e - 2))
                    nc.vector.tensor_tensor(dec[:, e % 2], b[:, :, P - 1:P].broadcast_to([P, HEADS, P]), b,
                                            ALU.subtract).then_inc(gap_ready.sem, 1)

                def silu(f):
                    name, row = ("r", f), scratch[:, f % 2, :]
                    dve.wait_ge(*gate_tanh_ready.at(n, f))
                    link(nc.vector.tensor_scalar(row, row, 1.0, half_gain_o[:, f % 2:f % 2 + 1], ALU.add, ALU.mult))
                    nc.vector.tensor_tensor(sr[:, f, :], bank(name), row, ALU.mult)\
                        .then_inc(bank_read[bank_of(name)], 1)

                def take_level(c, level):
                    name = ("level", c, level)
                    a = heads_of(xq_a[:, c, :])
                    dve.wait_ge(*full(n, name))
                    if level == 0:
                        nc.vector.tensor_tensor(a, heads_of(bank(name)),
                                                ident[:].unsqueeze(1).broadcast_to([P, HEADS, P]), ALU.mult)\
                            .then_inc(bank_read[bank_of(name)], 1)
                    else:
                        w = WIDTHS[level - 1]
                        mask = masks[:, level - 1, :].unsqueeze(1).broadcast_to([P, HEADS, HALF])
                        dve.wait_ge(*read(n, ("level", c, level - 1)))
                        link(nc.vector.nop())
                        nc.vector.copy_predicated(spans(a, w, True), packed(mask, w),
                                                  packed(heads_of(bank(name)[:, 0:HEADS * HALF]), w))\
                            .then_inc(bank_read[bank_of(name)], 1)

                next_chunk(0)
                dve.wait_ge(*full(n, "g"))
                nc.vector.tensor_copy(gT, bank("g")[0:RANK, :]).then_inc(bank_read[bank_of("g")], 1)
                next_chunk(1)
                next_chunk(C_Q)
                for h in range(HEADS):
                    dve.wait_ge(*soft_ready.at(n, h))
                    link(nc.vector.scalar_tensor_tensor(out=soft[:, h, :], in0=b_[:, h, :], scalar=0.0,
                                                        in1=soft[:, h, :], op0=ALU.min, op1=ALU.subtract))
                    last = nc.vector.tensor_tensor_scan(b_[:, h, :], scanm[:], soft[:, h, :], 0.0,
                                                        ALU.mult, ALU.add)
                last.then_inc(b_ready.sem, 1)
                dve.wait_ge(*b_ready.at(n, 0))
                attention_top(0)
                attention_norm(0)
                for i in range(C_Q + 1, C_V):
                    next_chunk(i)
                    if i >= C_K:
                        copy_k(2 * (i - C_K))
                        attention_low(i - C_K)
                        copy_k(2 * (i - C_K) + 1)
                    attention_top(i - C_Q)
                    attention_norm(i - C_Q)

                def update_state(c):
                    dve.wait_ge(*chunk_decay_ready.at(n, c))
                    if c:
                        dve.wait_ge(*full(n, ("o", c - 1, 1)))
                        dve.wait_ge(*read(n, ("su", c - 1, 1)))
                    for p in range(2):
                        dve.wait_ge(*full(n, ("su", c, p)))
                        for h in (2 * p, 2 * p + 1):
                            last = nc.vector.scalar_tensor_tensor(
                                out=states[(c + 1) % 2][:, h, :], in0=states[c % 2][:, h, :],
                                scalar=chunk_decay[:, c, h:h + 1],
                                in1=bank(("su", c, p))[:, (h % 2) * DV:(h % 2 + 1) * DV],
                                op0=ALU.mult, op1=ALU.add)
                        last.then_inc(bank_read[bank_of(("su", c, p))], 1)

                def o_mean_square(c):
                    dve.wait_ge(*o_ssq_ready.at(n, c))
                    nc.vector.tensor_scalar(o_ms[:, c, :], o_ssq[:, c, :], 1.0 / DV, EPS, ALU.mult, ALU.add)\
                        .then_inc(o_ms_ready.sem, 1)

                def gate_output(c, p):
                    dve.wait_ge(*full(n, ("oT", c, p)))
                    if p:
                        dve.wait_ge(*mix_ready.at(n, c))
                    nc.vector.tensor_tensor(heads_of(y_row(c)), heads_of(bank(("oT", c, p))),
                                            at_chunk(sr[:, 4 * p:4 * p + 4, :], c), ALU.mult)\
                        .then_inc(bank_read[bank_of(("oT", c, p))], 1)

                level_gap(0, 1)
                for hs in range(STEPS):
                    i, c = C_V + hs // 2, hs // 4
                    if hs:
                        for level in levels_of(hs - 1):
                            take_level((hs - 1) // 4, level)
                    if hs % 4 == 0 and c:
                        level_gap(c, 1)
                    if hs % 2 == 0:
                        next_chunk(i)
                    if hs in (1, 3):
                        attention_low(2 + hs // 2)
                    if hs in (10, 12, 14):
                        update_state(hs // 2 - 5)
                    if hs >= 9:
                        silu(hs - 9)
                    if hs % 4 == 3:
                        end_gap(c)
                    else:
                        for level in levels_of(hs + 1):
                            level_gap(c, level)
                    if hs in (10, 12, 14):
                        o_mean_square(hs // 2 - 5)

                for level in levels_of(STEPS - 1):
                    take_level(TILES - 1, level)
                silu(KD - 1)
                next_chunk(C_OUT)
                o_mean_square(TILES - 1)
                for c in range(TILES):
                    gate_output(c, 0)
                next_chunk(C_OUT + 1)
                update_state(TILES - 1)
                for c in range(TILES):
                    gate_output(c, 1)

                def add_out(name, t, cols, more=0):
                    dve.wait_ge(*full(n, name, more))
                    nc.vector.tensor_tensor(xres[:, t, cols], bank(name), xres[:, t, cols], ALU.add)\
                        .then_inc(bank_read[bank_of(name)], 1)

                def norm_ms(which, t):
                    dve.wait_ge(*ssq_ready.at(n, which * TILES + t))
                    mean_square(which, t)

                def norm_scale(which, t, source, to):
                    dve.wait_ge(*rstd_ready.at(n, which * TILES + t))
                    scale_tile(which, t, source, to)

                def h_low(h, g):
                    dve.wait_ge(*hi_part.at(n, 2 * TILES + h * (KD // 2) + g))
                    for j in range(2):
                        at, part = slice(h * 256, (h + 1) * 256), slice(j * 256, (j + 1) * 256)
                        last = nc.vector.scalar_tensor_tensor(
                            out=h_lo[:, 2 * g + j, at], in0=bank(("hT", h, g))[:, part],
                            scalar=gain_mlp[:, 2 * g + j:2 * g + j + 1], in1=h_hi[:, 2 * g + j, at].bitcast(F32),
                            op0=ALU.mult, op1=ALU.subtract)
                    last.then_inc(bank_read[bank_of(("hT", h, g))], 1)

                for i in range(C_OUT + 2, C_UP[0]):
                    next_chunk(i)
                    if i == C_OUT + 2:
                        dve.wait_ge(*xres_loaded.at(n, 0))
                        for t in range(TILES):
                            add_out(("out", 0, t), t, slice(0, 512))
                second = slice(512, 1024)
                add_out(("out", 1, 0), 0, second)
                norm_ms(0, 0)
                for t in range(1, TILES):
                    add_out(("out", 1, t), t, second)
                    norm_scale(0, t - 1, xres, hn)
                    if t < TILES - 1:
                        norm_ms(0, t)
                h_low(0, 0)
                h_low(0, 1)
                norm_ms(0, TILES - 1)
                h_low(0, 2)
                norm_scale(0, TILES - 1, xres, hn)
                h_low(0, 3)
                for g in range(KD // 2):
                    h_low(1, g)
                restart()

                def final_scale(t):
                    dve.wait_ge(*rstd_ready.at(n, 2 * TILES + t))
                    nc.vector.scalar_tensor_tensor(out=xres[:, t, :], in0=xres[:, t, :], scalar=rstd[:, 2, t:t + 1],
                                                   in1=gain_fin[:], op0=ALU.mult, op1=ALU.mult)\
                        .then_inc(out_ready.sem, 1)

                for half in range(2):
                    with dve.Fori(0, UF // 4) as j:
                        for c in range(2):
                            i = C_UP[half] + c
                            split_lo(n, j * 2 + (i + 1), (i + 1) % 2)
                            for f in range(2):
                                at = bass.ds(j * 4 + (2 * c + f), 1)
                                dve.wait_ge(*square_ready.at(n, j * 4 + (half * UF + 2 * c + f)))
                                row = scratch[:, f:f + 1, :]
                                link(nc.vector.tensor_copy(u_hi[:, at, :], row))
                                nc.vector.tensor_tensor(u_lo[:, at, :], row, u_hi[:, at, :].bitcast(F32),
                                                        ALU.subtract).then_inc(u_ready.sem, 1)
                        restart()
                    if half == 0:
                        with dve.Fori(0, 2) as d:
                            for kg in range(UF // KG):
                                i = C_DOWN[0] + kg
                                split_lo(n, d * 4 + (i + 1), (i + 1) % 2)
                            for t in range(TILES):
                                add_out(("down", 0, 0, t), t, bass.ds(d * 512, 512), d)
                        for t in range(TILES):
                            norm_ms(1, t)
                        for t in range(TILES):
                            norm_scale(1, t, xin, xin)
                    else:
                        for d in range(2):
                            for kg in range(UF // KG):
                                i = C_DOWN[1] + 4 * d + kg
                                split_lo(n, i + 1, (i + 1) % 2)
                                k = 4 * d + kg
                                dve.wait_ge(*hi_part.at(n, 2 * TILES + KD + k))
                                low("xT", k, gain_mix)
                            for t in range(TILES):
                                add_out(("down", 1, d, t), t, slice(512 * d, 512 * (d + 1)))
                                if d == 1:
                                    if t >= 1:
                                        norm_ms(2, t - 1)
                                    if t >= 2:
                                        final_scale(t - 2)
                        norm_ms(2, TILES - 1)
                        final_scale(TILES - 2)
                        final_scale(TILES - 1)

        @block.tensor
        def _(pe):
            chunk_done = [False]

            def after_chunk(ins):
                if chunk_done[0]:
                    ins.then_inc(weights_used.sem, 1)
                chunk_done[0] = False

            def product(to, left, right, start, stop):
                after_chunk(pe.matmul(to, left[0], right[0], start=start, stop=False))
                pe.matmul(to, left[0], right[1], start=False, stop=False)
                return pe.matmul(to, left[1], right[0], start=False, stop=stop)

            def wait_weights(n, i):
                pe.wait_ge(*hi_split.at(n, i))
                pe.wait_ge(*lo_split.at(n, i))

            def feature_rows(slot, f, to, cols):
                wh, wl = as_kblocks(w_hi, slot, KD), as_kblocks(w_lo, slot, KD)
                for k in range(KD):
                    last = product(to, (wh[:, k, f * P:(f + 1) * P], wl[:, k, f * P:(f + 1) * P]),
                                   (h_hi[:, k, 0:cols], h_lo[:, k, 0:cols]), k == 0, k == KD - 1)
                return last

            def token_rows(slot, to, left, start, stop):
                wh, wl = as_kblocks(w_hi, slot, KG), as_kblocks(w_lo, slot, KG)
                for k in range(KG):
                    last = product(to, left(k), (wh[:, k, :], wl[:, k, :]), start and k == 0, stop and k == KG - 1)
                return last

            def transposes(name, source, tiles, k):
                for t in range(tiles):
                    last = pe.transpose(banks[:, bank_of((name, k)), t * P:(t + 1) * P],
                                        source[:, t, k * P:(k + 1) * P], ident[:])
                last.then_inc(bank_full[bank_of((name, k))], 1)

            pe.wait_ge(first_consts_loaded, 16 * 3)
            pe.wait_ge(*normed.early(MT - 1))
            for k in range(KD):
                if k >= 4:
                    pe.wait_ge(*early_empty(("memT", k)))
                transposes("memT", xres, MT, k)
            for k in range(KD - 4, KD):
                pe.wait_ge(*early_read(("memT", k)))
            for i in range(KV_CHUNKS):
                pe.wait_ge(*hi_split.early(i))
                pe.wait_ge(*lo_split.early(i))
                if i < 2:
                    for f in range(2):
                        name = ("km", 2 * i + f)
                        if i:
                            pe.wait_ge(*early_empty(name))
                        feature_rows(i % 2, f, bank(name)[:, 0:MEM], MEM).then_inc(bank_full[bank_of(name)], 1)
                else:
                    wh, wl = as_kblocks(w_hi, i % 2, KD), as_kblocks(w_lo, i % 2, KD)
                    for m in range(MT):
                        name = ("vm", i - 2, m)
                        if i == 3:
                            pe.wait_ge(*early_empty(name))
                        for k in range(KD):
                            at = slice(m * P, (m + 1) * P)
                            last = product(bank(name)[:, 0:FCOLS], (h_hi[:, k, at], h_lo[:, k, at]),
                                           (wh[:, k, :], wl[:, k, :]), k == 0, k == KD - 1)
                        last.then_inc(bank_full[bank_of(name)], 1)
                chunk_done[0] = True
            pe.wait_ge(*normed.early(MT + TILES - 1))
            for k in range(KD):
                pe.wait_ge(*early_empty(("x0T", k)))
                transposes("x0T", xin, TILES, k)
            for k in range(KD - 4, KD):
                pe.wait_ge(*early_read(("x0T", k)))
            pe.wait_ge(wg_ready, 1)

            with pe.Fori(0, BLOCKS) as n:
                def feature_part(i, f, name):
                    if f == 0:
                        wait_weights(n, i)
                    pe.wait_ge(*empty(n, name))
                    feature_rows(i % 2, f, bank(name), BLOCK).then_inc(bank_full[bank_of(name)], 1)
                    chunk_done[0] = f == 1

                def gate_features():
                    pe.wait_ge(*empty(n, "g"))
                    for k in range(KD):
                        last = product(bank("g")[0:RANK, :], (wg_hi[:, k, :], wg_lo[:, k, :]),
                                       (h_hi[:, k, :], h_lo[:, k, :]), k == 0, k == KD - 1)
                    last.then_inc(bank_full[bank_of("g")], 1)

                def gate_logits():
                    pe.wait_ge(*read(n, "g"))
                    for h in range(HEADS):
                        pe.wait_ge(*empty(n, ("z", h)))
                        pe.matmul(bank(("z", h)), w2[:, h * DK:(h + 1) * DK], gT, start=True, stop=True)\
                            .then_inc(bank_full[bank_of(("z", h))], 1)

                def scores(t):
                    for p in range(2):
                        pe.wait_ge(*empty(n, ("score", t, p)))
                        if t == 0:
                            for h in (2 * p, 2 * p + 1):
                                pe.wait_ge(*read(n, ("xq", h)))
                        for h in (2 * p, 2 * p + 1):
                            last = pe.matmul(bank(("score", t, p))[:, (h % 2) * MEM:(h % 2 + 1) * MEM],
                                             xq_a[:, h, t * P:(t + 1) * P], kmT[:, h, :], start=True, stop=True)
                            if h == 0:
                                after_chunk(last)
                        last.then_inc(bank_full[bank_of(("score", t, p))], 1)

                def probs_transposes(t):
                    for p in range(2):
                        name = ("pT", t, p)
                        pe.wait_ge(*empty(n, name))
                        pe.wait_ge(*probs_ready.at(n, 2 * t + p))
                        for j in range(4):
                            at = (4 * p + j) * P
                            last = pe.transpose(bank(name)[:, j * P:(j + 1) * P], probs[:, t % 2, at:at + P], ident[:])
                        last.then_inc(bank_full[bank_of(name)], 1)

                def attention_values(t):
                    for p in range(2):
                        name = ("pv", t, p)
                        pe.wait_ge(*empty(n, name))
                        pe.wait_ge(*read(n, ("pT", t, p)))
                        for h in (2 * p, 2 * p + 1):
                            for m in range(MT):
                                last = pe.matmul(bank(name)[:, (h % 2) * P:(h % 2 + 1) * P], vm[:, m, h * P:(h + 1) * P],
                                                 probsT[:, t % 2, (h * MT + m) * P:(h * MT + m + 1) * P],
                                                 start=m == 0, stop=m == MT - 1)
                        last.then_inc(bank_full[bank_of(name)], 1)

                def level_scores(c, level):
                    name = ("level", c, level)
                    pe.wait_ge(*empty(n, name))
                    if level == 0:
                        if c == 0:
                            for f in range(2):
                                pe.wait_ge(*read(n, ("k", 2 + f)))
                    else:
                        pe.wait_ge(*product_ready.at(n, c * DECAYS + level - 1))
                    for h in range(HEADS):
                        plain = level == 0 or WIDTHS[level - 1] == 1
                        left = k_[:, h, c * P:(c + 1) * P] if plain else keys[:, level % 2, h, :]
                        if level == 0:
                            ins = pe.matmul(bank(name)[:, h * P:(h + 1) * P], left, q[:, h, c * P:(c + 1) * P],
                                            start=True, stop=True)
                        else:
                            ins = pe.matmul(bank(name)[:, h * HALF:(h + 1) * HALF], left, queries[:, level % 2, h, :],
                                            start=True, stop=True)
                        if h == 0:
                            after_chunk(ins)
                    ins.then_inc(bank_full[bank_of(name)], 1)

                def state_step(what, c):
                    if what == "kT":
                        name = ("kT", c)
                        pe.wait_ge(*empty(n, name))
                        pe.wait_ge(*product_ready.at(n, c * DECAYS + KEY_DECAY))
                        for h in range(HEADS):
                            last = pe.transpose(bank(name)[:, h * P:(h + 1) * P], k_[:, h, c * P:(c + 1) * P], ident[:])
                            if h == 0:
                                after_chunk(last)
                        last.then_inc(bank_full[bank_of(name)], 1)
                    elif what == "su":
                        pe.wait_ge(*read(n, ("kT", c)))
                        for p in range(2):
                            name = ("su", c, p)
                            pe.wait_ge(*empty(n, name))
                            pe.wait_ge(*read(n, ("v", p, c)))
                            for h in (2 * p, 2 * p + 1):
                                last = pe.matmul(bank(name)[:, (h % 2) * DV:(h % 2 + 1) * DV],
                                                 k_[:, h, c * P:(c + 1) * P], v[:, c, h * DV:(h + 1) * DV],
                                                 start=True, stop=True)
                            last.then_inc(bank_full[bank_of(name)], 1)
                    else:
                        pe.wait_ge(*read(n, ("level", c, LEVELS - 1)))
                        pe.wait_ge(*read(n, ("level", c, LEVELS - 2)))
                        pe.wait_ge(*product_ready.at(n, c * DECAYS + QUERY_DECAY))
                        for p in range(2):
                            name = ("o", c, p)
                            pe.wait_ge(*empty(n, name))
                            if c:
                                pe.wait_ge(*read(n, ("su", c - 1, p)))
                            for h in (2 * p, 2 * p + 1):
                                to = bank(name)[:, (h % 2) * DV:(h % 2 + 1) * DV]
                                pe.matmul(to, xq_a[:, c, h * P:(h + 1) * P], v[:, c, h * DV:(h + 1) * DV],
                                          start=True, stop=False)
                                last = pe.matmul(to, q[:, h, c * P:(c + 1) * P], states[c % 2][:, h, :],
                                                 start=False, stop=True)
                            last.then_inc(bank_full[bank_of(name)], 1)

                def output_transposes(c, p):
                    name = ("oT", c, p)
                    pe.wait_ge(*empty(n, name))
                    pe.wait_ge(*read(n, ("o", c, 1)))
                    if p == 0:
                        pe.wait_ge(*read(n, ("o", c, 0)))
                    for j in range(4):
                        at = (4 * p + j) * P
                        last = pe.transpose(bank(name)[:, j * P:(j + 1) * P], o_n[c][:, at:at + P], ident[:])
                        if j == 0:
                            after_chunk(last)
                    last.then_inc(bank_full[bank_of(name)], 1)

                def out_tile(i, t):
                    d, kg = (i - C_OUT) // 3, OUT_ORDER[(i - C_OUT) % 3]
                    name, at = ("out", d, t), slice(t * P, (t + 1) * P)
                    if t == 0:
                        wait_weights(n, i)
                    if kg == OUT_ORDER[0]:
                        pe.wait_ge(*empty(n, name))
                    hi, lo, k0 = (h_hi, h_lo, KG * kg) if kg < 2 else (mem_hi, mem_lo, 0)
                    last = token_rows(i % 2, bank(name), lambda k: (hi[:, k0 + k, at], lo[:, k0 + k, at]),
                                      kg == OUT_ORDER[0], kg == OUT_ORDER[2])
                    if kg == OUT_ORDER[2]:
                        last.then_inc(bank_full[bank_of(name)], 1)
                    chunk_done[0] = t == TILES - 1

                for b in (6, 7):
                    pe.wait_ge(bank_read[b], n * USES.count[b] + EARLY.count[b])
                feature_part(0, 0, ("xq", 0))
                feature_part(0, 1, ("xq", 1))
                gate_features()
                feature_part(1, 0, ("xq", 2))
                feature_part(1, 1, ("xq", 3))
                gate_logits()
                for i in range(C_Q, C_V):
                    for f in range(2):
                        feature_part(i, f, ("q", 2 * (i - C_Q) + f) if i < C_K else ("k", 2 * (i - C_K) + f))
                        if f == 0 and i >= C_K:
                            attention_values(i - C_K)
                    scores(i - C_Q)
                    if i > C_Q:
                        probs_transposes(i - C_Q - 1)
                for hs in range(STEPS):
                    i, f = C_V + hs // 2, hs % 2
                    if i < C_R:
                        d, kg = divmod(i - C_V, 2)
                        if f == 0:
                            wait_weights(n, i)
                        for t in (2 * f, 2 * f + 1):
                            if kg == 0:
                                pe.wait_ge(*empty(n, ("v", d, t)))
                            at = slice(t * P, (t + 1) * P)
                            last = token_rows(i % 2, bank(("v", d, t)),
                                              lambda k: (h_hi[:, KG * kg + k, at], h_lo[:, KG * kg + k, at]),
                                              kg == 0, kg == 1)
                            if kg == 1:
                                last.then_inc(bank_full[bank_of(("v", d, t))], 1)
                        chunk_done[0] = f == 1
                    else:
                        feature_part(i, f, ("r", hs - 8))
                    if hs == 0:
                        probs_transposes(TILES - 1)
                    if hs in (0, 2):
                        attention_values(2 + hs // 2)
                    for level in levels_of(hs):
                        level_scores(hs // 4, level)
                    for what, c in STATE_STEPS.get(hs, ()):
                        state_step(what, c)

                for p in range(2):
                    pe.wait_ge(*read(n, ("pv", TILES - 1, p)))
                out_tile(C_OUT, 0)
                out_tile(C_OUT, 1)
                state_step("o", TILES - 1)
                state_step("kT", TILES - 1)
                out_tile(C_OUT, 2)
                for c in range(TILES - 1):
                    output_transposes(c, 0)
                out_tile(C_OUT, 3)
                output_transposes(TILES - 1, 0)
                state_step("su", TILES - 1)
                for t in range(TILES):
                    if t == 2:
                        for c in range(TILES):
                            output_transposes(c, 1)
                    pe.wait_ge(*mix_ready.at(n, t))
                    out_tile(C_OUT + 1, t)
                for t in range(TILES):
                    pe.wait_ge(*mix_ready.at(n, TILES + t))
                    out_tile(C_OUT + 2, t)
                for i in range(C_OUT + 3, C_UP[0]):
                    for t in range(TILES):
                        out_tile(i, t)

                def h_transposes(h):
                    pe.wait_ge(*normed.at(n, 2 * h + 1))
                    for g in range(KD // 2):
                        name = ("hT", h, g)
                        pe.wait_ge(*empty(n, name))
                        for j in range(2):
                            for t in range(2):
                                last = pe.transpose(bank(name)[:, (2 * j + t) * P:(2 * j + t + 1) * P],
                                                    hn[:, 2 * h + t, (2 * g + j) * P:(2 * g + j + 1) * P], ident[:])
                        last.then_inc(bank_full[bank_of(name)], 1)

                def up_chunk(half, c, j):
                    wait_weights(n, j * 2 + (C_UP[half] + c))
                    for f in range(2):
                        pe.wait_ge(*empty(n, ("up", half, c, f), j * 2))
                        feature_rows(c, f, banks[:, f, :], BLOCK).then_inc(bank_full[f], 1)
                    chunk_done[0] = True

                def down_columns(half, d):
                    for kg in range(UF // KG):
                        wait_weights(n, d * 4 + (C_DOWN[half] + kg))
                        pe.wait_ge(*u_ready.at(n, half * UF + KG * (kg + 1) - 1))
                        for t in range(TILES):
                            name, at = ("down", half, 0, t), slice(t * P, (t + 1) * P)
                            if kg == 0:
                                pe.wait_ge(*empty(n, name, d))
                            last = token_rows(kg % 2, bank(name),
                                              lambda k: (u_hi[:, KG * kg + k, at], u_lo[:, KG * kg + k, at]),
                                              kg == 0, kg == UF // KG - 1)
                            if kg == UF // KG - 1:
                                last.then_inc(bank_full[bank_of(name)], 1)
                            if half == 1 and t == 1:
                                pe.wait_ge(*normed.at(n, 2 * TILES - 1))
                                pe.wait_ge(*empty(n, ("xT", 4 * d + kg)))
                                transposes("xT", xin, TILES, 4 * d + kg)
                        chunk_done[0] = True

                h_transposes(0)
                wait_weights(n, C_UP[0])
                wh, wl = as_kblocks(w_hi, 0, KD), as_kblocks(w_lo, 0, KD)
                for h in range(2):
                    at = slice(h * 256, (h + 1) * 256)
                    for g in range(KD // 2):
                        pe.wait_ge(*read(n, ("hT", h, g)))
                        for f in range(2):
                            if h == 0 and g == 0:
                                pe.wait_ge(*empty(n, ("up", 0, 0, f)))
                            for k in (2 * g, 2 * g + 1):
                                last = product(banks[:, f, at],
                                               (wh[:, k, f * P:(f + 1) * P], wl[:, k, f * P:(f + 1) * P]),
                                               (h_hi[:, k, at], h_lo[:, k, at]), k == 0, k == KD - 1)
                            if h == 1 and g == KD // 2 - 1:
                                last.then_inc(bank_full[f], 1)
                    if h == 0:
                        h_transposes(1)
                chunk_done[0] = True
                up_chunk(0, 1, 0)

                for half in range(2):
                    with pe.Fori(1 - half, UF // 4) as j:
                        for c in range(2):
                            up_chunk(half, c, j)
                    if half == 0:
                        with pe.Fori(0, 2) as d:
                            down_columns(0, d)
                    else:
                        for d in range(2):
                            down_columns(1, d)


IN_NAMES = ["x", "mem", "norm_mix", "norm_mem", "w_kv", "w_out", "norm_mlp", "w_up", "w_down", "gla_w_in",
            "gla_w_gate2", "gla_b_gate", "gla_out_gain", "final_norm"]

BY_PARTITION = ("norm_mix", "norm_mem", "norm_mlp", "gla_b_gate", "gla_out_gain")


def shape_constants():
    s = np.arange(P)
    t = np.arange(P)
    masks = np.zeros((P, len(WIDTHS), HALF), np.float32)
    for n, w in enumerate(WIDTHS):
        upper = t[t // w % 2 == 1]
        masks[:, n, :] = (s[:, None] // (2 * w) == upper[None, :] // (2 * w)) & (s[:, None] // w % 2 == 0)
    scan = np.ones((P, BLOCK), np.float32)
    scan[:, ::P] = 0
    return {"level_masks": masks.reshape(P, -1), "identity": np.eye(P, dtype=np.float32), "scan_mask": scan}


def kernel(**inputs):
    import concourse.bacc as bacc
    from concourse.bass_utils import run_bass_kernel_spmd

    nc = bacc.Bacc("TRN2", target_bir_lowering=False, num_devices=1)
    arrays, args = {}, []

    def give(name, a):
        a = np.ascontiguousarray(a)
        arrays[name] = a
        args.append(nc.dram_tensor(name, a.shape, mybir.dt.from_np(a.dtype), kind="ExternalInput").ap())

    for name in IN_NAMES:
        a = np.asarray(inputs[name])
        a = a if name == "final_norm" else a[0]
        if name in BY_PARTITION:
            a = a.reshape(-1, P).T
        give(f"in_{name}", a)
    for name, a in shape_constants().items():
        give(name, a)
    out = nc.dram_tensor("out", (SEQ, D), F32, kind="ExternalOutput").ap()
    build(nc, *args, out)
    r = run_bass_kernel_spmd(nc, [arrays], core_ids=[0])
    return r.results[0]["out"].reshape(1, SEQ, D)
```

```python
from contextlib import ExitStack

import numpy as np

import concourse.bass as bass
from concourse import mybir

F32 = mybir.dt.float32
F32R = mybir.dt.float32r
BF16 = mybir.dt.bfloat16
U8 = mybir.dt.uint8
ALU = mybir.AluOpType
ACT = mybir.ActivationFunctionType
AX_X = mybir.AxisListType.X

P = 128
D = 1024
KD = D // P
SEQ = 2048
BLOCK = 512
BLOCKS = SEQ // BLOCK
TILES = BLOCK // P
MEM = 256
MT = MEM // P
HEADS = 4
DK = 128
DV = 256
RANK = 16
PAIR = 2 * RANK
TAU = 16.0
XH = 4
XD = XH * P
HIDDEN = 4 * D
EPS = 1e-6
QSCALE = DK ** -0.5
XSCALE = P ** -0.5

COL_Q = 0
COL_K = COL_Q + HEADS * DK
COL_V = COL_K + HEADS * DK
COL_G = COL_V + HEADS * DV
COL_R = COL_G + RANK
COL_XQ = COL_R + D

SPANS = [32, 8, 2]
RUNGS = len(SPANS) + 1
NEAR = 0
KINDS = [(1, 3, 0), (2, 2, 96), (3, 1, 160)]
COLS = 192
ODD = P // 2
QUERY_DECAY = RUNGS - 1
KEY_DECAY = QUERY_DECAY + 1
DECAYS = KEY_DECAY + 1

CHUNK = 2048
FCOLS = CHUNK // KD
KG = 4
C_XQ, C_Q, C_K, C_V, C_R = 0, 2, 4, 6, 10
C_OUT = C_R + 4
OUT_ORDER = (2, 0, 1)
C_UP = [C_OUT + 6, C_OUT + 6 + 16]
C_DOWN = [C_UP[0] + 8, C_UP[1] + 8]
CHUNKS = C_DOWN[1] + 8
KV_CHUNKS = 4
HALF_HIDDEN = HIDDEN // 2
UF = HALF_HIDDEN // P
STEPS = 2 * (C_OUT - C_V)


class Signal:

    def __init__(self, sem, before, per_block, step=1):
        self.sem, self.before, self.per_block, self.step = sem, before, per_block, step

    def at(self, n, k):
        return self.sem, n * (self.per_block * self.step) + (self.before + k + 1) * self.step

    def early(self, k):
        return self.sem, (k + 1) * self.step


class UseOrder:

    def __init__(self, uses):
        self.count = [0] * 8
        self.place = {}
        for bank, name in uses:
            self.place[name] = (bank, self.count[bank])
            self.count[bank] += 1


EARLY_RING = (6, 7, 4, 5, 2, 3)


def early_uses():
    for k in range(KD):
        yield EARLY_RING[k % len(EARLY_RING)], ("memT", k)
    for h in range(XH):
        yield h % 2, ("km", h)
    for c in range(2):
        for m in range(MT):
            yield 2 + m, ("vm", c, m)
    for k in range(KD):
        yield EARLY_RING[k % len(EARLY_RING)], ("x0T", k)


def block_uses():
    for h in range(XH):
        yield h % 2, ("xq", h)
    yield 2, "g"
    for h in range(HEADS):
        yield (4, 5, 3, 2)[h], ("z", h)
    for f in range(4):
        yield f % 2, ("q", f)
        if f % 2:
            for use in attention_uses(C_Q + f // 2):
                yield use
    for f in range(4):
        yield f % 2, ("k", f)
        if f % 2 == 0:
            for p in range(2):
                yield 4 + p, ("pv", f // 2, p)
        else:
            for use in attention_uses(C_K + f // 2):
                yield use
    for hs in range(STEPS):
        if hs < 8:
            if hs // 2 % 2 == 0:
                for t in (2 * (hs % 2), 2 * (hs % 2) + 1):
                    yield 2 + t, ("v", hs // 4, t)
        else:
            yield hs % 2, ("r", hs - 8)
        if hs == 0:
            for p in range(2):
                yield 6 + p, ("pT", TILES - 1, p)
        if hs in (0, 2):
            for p in range(2):
                yield p, ("pv", 2 + hs // 2, p)
        for p in range(2):
            yield 6 + p, ("rung", hs // 4, hs % 4, p)
        for what, c in STATE_STEPS.get(hs, ()):
            for use in state_uses(what, c):
                yield use
    for what, c in (("o", 3), ("kT", 3), ("oT", (0, 0)), ("oT", (1, 0)), ("oT", (2, 0)), ("oT", (3, 0)), ("su", 3),
                    ("oT", (0, 1)), ("oT", (1, 1)), ("oT", (2, 1)), ("oT", (3, 1))):
        for use in state_uses(what, c):
            yield use
    for d in range(2):
        for t in range(TILES):
            yield 2 + t, ("out", d, t)
    for g in range(KD // 2):
        yield (6, 7, 2, 3)[g], ("hT", 0, g)
    for g in range(KD // 2):
        yield 4 + g, ("hT", 1, g)
    for half in range(2):
        for c in range(UF // 2):
            for f in range(2):
                yield f, ("up", half, c, f)
        for d in range(2):
            for t in range(TILES):
                yield 2 + t, ("down", half, d, t)
    for k in range(KD):
        yield 6 + k % 2, ("xT", k)


def attention_uses(i):
    for p in range(2):
        yield 2 + p, ("score", i - C_Q, p)
    if i > C_Q:
        for p in range(2):
            yield 6 + p, ("pT", i - C_Q - 1, p)


def state_uses(what, c):
    last = c == TILES - 1
    if what == "kT":
        yield 0 if last else 2, ("kT", c)
    elif what == "su":
        for p in range(2):
            yield (6 + p if last else 3 - p), ("su", c, p)
    elif what == "o":
        for p in range(2):
            yield (6 + p if last else 4 + p), ("o", c, p)
    else:
        yield c[0] % 2, ("oT",) + c


STATE_STEPS = {8: [("kT", 0)], 9: [("su", 0), ("o", 0)], 10: [("kT", 1)], 11: [("su", 1), ("o", 1)],
               12: [("kT", 2)], 13: [("su", 2), ("o", 2)]}

EARLY = UseOrder(early_uses())
USES = UseOrder(block_uses())


def build(nc, x, mem, norm_mix, norm_mem, w_kv, w_out, norm_mlp, w_up, w_down, w_in, w_gate2, b_gate,
          out_gain, final_norm, rung_masks, identity, scan_mask, out):
    with ExitStack() as ctx:
        def sb(name, shape, dt=F32):
            return ctx.enter_context(nc.sbuf_tensor(name, shape, dt))

        def sem(name):
            return ctx.enter_context(nc.semaphore(name))

        h_hi = sb("h_hi", [P, KD, BLOCK], F32R)
        h_lo = sb("h_lo", [P, KD, BLOCK], F32R)
        raw = sb("raw", [P, 2, CHUNK])
        w_hi = sb("w_hi", [P, 2, CHUNK], F32R)
        w_lo = sb("w_lo", [P, 2, CHUNK], F32R)
        kmT = sb("kmT", [P, XH, MEM])
        vm = sb("vm", [P, MT, XD])
        carried_state = sb("carried_state", [P, HEADS, DV])
        scratch = sb("scratch", [P, 2, BLOCK])
        keys = sb("keys", [P, HEADS, P])
        gain_fin = sb("gain_fin", [P, D])
        w2_parts = sb("w2_parts", [3 * PAIR, HEADS * DK], F32R)
        ident = sb("ident", [P, P])
        masks = sb("masks", [P, (RUNGS - 1) * COLS + ODD], U8)
        scanm = sb("scanm", [P, BLOCK], U8)
        wg_pair = sb("wg_pair", [P, KD, PAIR], F32R)
        gain_mem = sb("gain_mem", [P, KD])
        gain_mix = sb("gain_mix", [P, KD])
        gain_mlp = sb("gain_mlp", [P, KD])
        gate_bias = sb("gate_bias", [P, HEADS])
        gain_o = sb("gain_o", [P, DV // P])
        half_gain_o = sb("half_gain_o", [P, DV // P])
        minus_half = sb("minus_half", [P, HEADS])
        ssq = sb("ssq", [P, 3, TILES])
        ms = sb("ms", [P, 3, TILES])
        rstd = sb("rstd", [P, 3, TILES])
        o_ssq = sb("o_ssq", [P, TILES, HEADS])
        o_ms = sb("o_ms", [P, TILES, HEADS])
        o_rstd = sb("o_rstd", [P, TILES, HEADS])
        chunk_decay = sb("chunk_decay", [P, TILES, HEADS])
        top = sb("top", [P, TILES, XH])
        neg_top = sb("neg_top", [P, TILES, XH])
        den = sb("den", [P, TILES, XH])
        rden = sb("rden", [P, TILES, XH])

        with ExitStack() as mixers:
            def mx(name, shape, dt=F32):
                return mixers.enter_context(nc.sbuf_tensor(name, shape, dt))

            q = mx("q", [P, HEADS, BLOCK])
            k_ = mx("k", [P, HEADS, BLOCK])
            b_ = mx("b", [P, HEADS, BLOCK])
            xq_a = mx("xq_a", [P, TILES, BLOCK])
            v = mx("v", [P, TILES, D])
            key_dec = mx("key_dec", [P, HEADS, P])
            query_dec = mx("query_dec", [P, HEADS, COLS])
            queries = mx("queries", [P, HEADS, COLS])
            near_dec = mx("near_dec", [P, HEADS, ODD])
            y_rows = mx("y_rows", [P, 2, BLOCK])
            inner_state = mx("inner_state", [P, HEADS, DV])
            o_junk = mx("o_junk", [P, HEADS, DV], BF16)
            sr = mx("sr", [P, KD, BLOCK])
            mem_hi = mx("mem_hi", [P, XH, BLOCK], F32R)
            mem_lo = mx("mem_lo", [P, XH, BLOCK], F32R)
        with ExitStack() as mlp:
            u_hi = mlp.enter_context(nc.sbuf_tensor("u_hi", [P, UF, BLOCK], F32R))
            u_lo = mlp.enter_context(nc.sbuf_tensor("u_lo", [P, UF, BLOCK], F32R))
            xres = mlp.enter_context(nc.sbuf_tensor("xres", [P, TILES, D], F32))
            xin = mlp.enter_context(nc.sbuf_tensor("xin", [P, TILES, D], F32))
        with ExitStack() as norm:
            hn = norm.enter_context(nc.sbuf_tensor("hn", [P, TILES, D], F32))
        states = [carried_state, inner_state]
        probs, probsT = v[:, 0:2, :], v[:, 2:4, :]
        g_parts = mem_hi[0:3 * PAIR, 0, :]
        soft = sr[:, 0:HEADS, :]
        o_n = [v[:, c, :] for c in range(TILES - 1)] + [q[:].rearrange("p h t -> p (h t)")[:, 0:D]]
        w2_raw = b_[0:3 * PAIR, 0, :]
        masks_raw = query_dec[:].rearrange("p h t -> p (h t)")[:, 0:(RUNGS - 1) * COLS + ODD]
        scan_raw = scratch[:, 1, :]
        wg_raw = scratch[:, 0, 0:KD * RANK].rearrange("p (k c) -> p k c", k=KD)

        banks = ctx.enter_context(nc.psum_tensor("banks", [P, 8, 512], F32))

        bank_full = [sem(f"bank_full{b}") for b in range(8)]
        bank_read = [sem(f"bank_read{b}") for b in range(8)]
        raw_loaded = [Signal(sem(f"raw_loaded{s}"), KV_CHUNKS // 2, CHUNKS // 2, 16) for s in range(2)]
        hi_split = Signal(sem("hi_split"), KV_CHUNKS, CHUNKS)
        lo_split = Signal(sem("lo_split"), KV_CHUNKS, CHUNKS)
        weights_used = Signal(sem("weights_used"), KV_CHUNKS, CHUNKS)
        first_consts_loaded = sem("first_consts_loaded")
        consts_loaded = sem("consts_loaded")
        w2_loaded = sem("w2_loaded")
        mem_loaded = sem("mem_loaded")
        xin_loaded = Signal(sem("xin_loaded"), 1, 1, 16)
        xres_loaded = Signal(sem("xres_loaded"), 0, 1, 16)
        out_stored = Signal(sem("out_stored"), 1, TILES, 16)
        ssq_ready = Signal(sem("ssq_ready"), MT + TILES, 3 * TILES)
        ms_ready = Signal(sem("ms_ready"), MT + TILES, 3 * TILES)
        rstd_ready = Signal(sem("rstd_ready"), MT + TILES, 3 * TILES)
        normed = Signal(sem("normed"), MT + TILES, 2 * TILES)
        hi_part = Signal(sem("hi_part"), 2 * KD, 2 * TILES + 2 * KD)
        minus_half_set = sem("minus_half_set")
        wg_hi_ready = sem("wg_hi_ready")
        g_hi_ready = Signal(sem("g_hi_ready"), 0, 1)
        wg_ready = sem("wg_ready")
        half_gain_ready = sem("half_gain_ready")
        soft_ready = Signal(sem("soft_ready"), 0, HEADS)
        soft_exp = Signal(sem("soft_exp"), 0, 1)
        b_ready = Signal(sem("b_ready"), 0, 1)
        top_ready = Signal(sem("top_ready"), 0, 2 * TILES)
        probs_ready = Signal(sem("probs_ready"), 0, 2 * TILES)
        gap_ready = Signal(sem("gap_ready"), 0, TILES * (DECAYS - 1))
        plain_ready = Signal(sem("plain_ready"), 0, TILES)
        near_gap = Signal(sem("near_gap"), 0, TILES)
        near_decay = Signal(sem("near_decay"), 0, TILES)
        near_product = Signal(sem("near_product"), 0, TILES)
        decay_ready = Signal(sem("decay_ready"), 0, TILES * DECAYS)
        product_ready = Signal(sem("product_ready"), 0, TILES * DECAYS)
        chunk_decay_ready = Signal(sem("chunk_decay_ready"), 0, TILES)
        gate_tanh_ready = Signal(sem("gate_tanh_ready"), 0, KD)
        o_ssq_ready = Signal(sem("o_ssq_ready"), 0, TILES)
        o_ms_ready = Signal(sem("o_ms_ready"), 0, TILES)
        o_rstd_ready = Signal(sem("o_rstd_ready"), 0, TILES)
        y_hi_ready = Signal(sem("y_hi_ready"), 0, 2 * TILES)
        mix_ready = Signal(sem("mix_ready"), 0, 2 * TILES)
        square_ready = Signal(sem("square_ready"), 0, 2 * UF)
        u_ready = Signal(sem("u_ready"), 2, 2 * UF)
        out_ready = Signal(sem("out_ready"), 0, TILES)
        dve_step = sem("dve_step")

        def full(n, name, more=0):
            bank, index = USES.place[name]
            return bank_full[bank], n * USES.count[bank] + more + (EARLY.count[bank] + index + 1)

        def empty(n, name, more=0):
            bank, index = USES.place[name]
            return bank_read[bank], n * USES.count[bank] + more + (EARLY.count[bank] + index)

        def read(n, name, more=0):
            bank, index = USES.place[name]
            return bank_read[bank], n * USES.count[bank] + more + (EARLY.count[bank] + index + 1)

        def early_full(name):
            bank, index = EARLY.place[name]
            return bank_full[bank], index + 1

        def early_empty(name):
            bank, index = EARLY.place[name]
            return bank_read[bank], index

        def early_read(name):
            bank, index = EARLY.place[name]
            return bank_read[bank], index + 1

        def bank_of(name):
            return (USES.place if name in USES.place else EARLY.place)[name][0]

        def bank(name):
            return banks[:, bank_of(name), :]

        def heads_of(ap, heads=HEADS):
            return ap.rearrange("p (h t) -> p h t", h=heads)

        def at_chunk(tensor, c):
            return tensor[:, :, c * P:(c + 1) * P]

        def odd(ap):
            return ap.rearrange("p h (s a) -> p h s a", a=2)[:, :, :, 1]

        def even(ap):
            return ap.rearrange("p h (s a) -> p h s a", a=2)[:, :, :, 0]

        def spans(ap, w, first, count):
            return ap.rearrange("p h (g x) -> p h g x", x=4 * w)[:, :, :, first * w:(first + count) * w]

        def span_end(ap, w, span, count):
            end = ap.rearrange("p h (g x) -> p h g x", x=4 * w)[:, :, :, (span + 1) * w - 1:(span + 1) * w]
            return end.broadcast_to([P, HEADS, P // (4 * w), count * w])

        def kind_cols(ap, w, kind):
            _, count, col = KINDS[kind]
            return ap[:, :, col:col + 32 * count].rearrange("p h (g x) -> p h g x", x=count * w)

        def rows(w):
            return w.rearrange("(k p) c -> p k c", p=P)

        win, wout, wup, wdown, wkv = rows(w_in), rows(w_out), rows(w_up), rows(w_down), rows(w_kv)
        x_tiles = x.rearrange("(t p) d -> p t d", p=P)
        out_tiles = out.rearrange("(t p) d -> p t d", p=P)
        mem_tiles = mem.rearrange("(t p) d -> p t d", p=P)
        first_cols = {C_XQ: COL_XQ, C_Q: COL_Q, C_K: COL_K, C_R: COL_R}

        def y_row(c):
            return scratch[:, c, :] if c < 2 else y_rows[:, c - 2, :]

        def chunk_source(i):
            i %= CHUNKS
            if i >= C_OUT:
                d, kg = (i - C_OUT) // 3, OUT_ORDER[(i - C_OUT) % 3]
                return wout[:, KG * kg:KG * (kg + 1), 512 * d:512 * (d + 1)]
            if C_V <= i < C_R:
                d, kg = divmod(i - C_V, 2)
                return win[:, KG * kg:KG * (kg + 1), COL_V + 512 * d:COL_V + 512 * (d + 1)]
            start = max(s for s in first_cols if s <= i)
            col = first_cols[start] + FCOLS * (i - start)
            return win[:, :, col:col + FCOLS]

        def as_kblocks(tensor, slot, kblocks):
            return tensor[:, slot, :].rearrange("p (k c) -> p k c", k=kblocks)

        block = ctx.enter_context(nc.Block())

        @block.sync
        def _(sp):
            def load(n, i, slot, source, kblocks):
                sp.wait_ge(*hi_split.at(n, i - 2))
                sp.wait_ge(*lo_split.at(n, i - 2))
                sp.dma_start(as_kblocks(raw, slot, kblocks), source).then_inc(raw_loaded[slot].sem, 16)

            sp.dma_start(xres[:, 0:MT, :], mem_tiles).then_inc(mem_loaded, 16)
            for i in range(KV_CHUNKS):
                if i >= 2:
                    sp.wait_ge(*hi_split.early(i - 2))
                    sp.wait_ge(*lo_split.early(i - 2))
                sp.dma_start(as_kblocks(raw, i % 2, KD), wkv[:, :, FCOLS * i:FCOLS * (i + 1)])\
                    .then_inc(raw_loaded[i % 2].sem, 16)
                if i == 1:
                    sp.dma_start(xin[:, :, :], x_tiles[:, 0:TILES, :]).then_inc(xin_loaded.sem, 16)
            load(0, 0, 0, chunk_source(0), KD)
            with sp.Fori(0, BLOCKS) as n:
                x_row = sp.snap(n * TILES)
                x_next = sp.snap(((n + 1) % BLOCKS) * TILES)
                for i in range(1, C_UP[0]):
                    load(n, i, i % 2, chunk_source(i), KD if i < C_V or C_R <= i < C_OUT else KG)
                    if i == C_OUT + 3:
                        sp.wait_ge(*read(n, ("oT", TILES - 1, 1)))
                        sp.dma_start(xres[:, :, :], x_tiles[:, bass.ds(x_row, TILES), :])\
                            .then_inc(xres_loaded.sem, 16)
                for half in range(2):
                    with sp.Fori(0, UF // 4) as j:
                        for c in range(2):
                            col = sp.snap(j * (2 * FCOLS) + (half * HALF_HIDDEN + c * FCOLS))
                            load(n, j * 2 + (C_UP[half] + c), c, wup[:, :, bass.ds(col, FCOLS)], KD)
                    if half == 0:
                        sp.wait_ge(*weights_used.at(n, C_UP[0] - 1))
                        sp.dma_start(xin[:, :, :], x_tiles[:, bass.ds(x_next, TILES), :])\
                            .then_inc(xin_loaded.sem, 16)
                    with sp.Fori(0, 2) as d:
                        col = sp.snap(d * 512)
                        for kg in range(UF // KG):
                            k0 = half * UF + KG * kg
                            load(n, d * 4 + (C_DOWN[half] + kg), kg % 2,
                                 wdown[:, k0:k0 + KG, bass.ds(col, 512)], KG)
                load(n, CHUNKS, 0, chunk_source(0), KD)

        @block.gpsimd
        def _(pool):
            nc.gpsimd.memset(minus_half[:], -0.5).then_inc(minus_half_set, 1)
            pool.wait_ge(minus_half_set, 1)

            def rsqrt(n, which, t):
                e = which * TILES + t
                pool.wait_ge(*ms_ready.at(n, e))
                nc.gpsimd.tensor_tensor(rstd[:, which, t:t + 1], ms[:, which, t:t + 1], minus_half[:, 0:1],
                                        ALU.pow).then_inc(rstd_ready.sem, 1)

            for e in range(MT + TILES):
                which, t = (0, e) if e < MT else (1, e - MT)
                if e == MT:
                    for tile, source in [(wg_raw, win[:, :, COL_G:COL_G + RANK]), (scan_raw, scan_mask),
                                         (masks_raw, rung_masks), (gain_o[:], out_gain), (gate_bias[:], b_gate),
                                         (gain_mlp[:], norm_mlp),
                                         (gain_fin[:], final_norm.rearrange("(a d) -> a d", a=1).broadcast_to([P, D]))]:
                        pool.dma_start(tile, source).then_inc(consts_loaded, 16)
                pool.wait_ge(*ms_ready.early(e))
                nc.gpsimd.tensor_tensor(rstd[:, which, t:t + 1], ms[:, which, t:t + 1], minus_half[:, 0:1],
                                        ALU.pow).then_inc(rstd_ready.sem, 1)

            def rung_products(n, c, rung):
                if rung:
                    pool.wait_ge(*full(n, ("rung", c, rung - 1, 1)))
                elif c:
                    pool.wait_ge(*full(n, ("rung", c - 1, RUNGS - 1, 1)))
                if rung == NEAR:
                    pool.wait_ge(*near_decay.at(n, c))
                    nc.gpsimd.tensor_tensor(queries[:, :, P:COLS], odd(at_chunk(q, c)), near_dec[:], ALU.mult)\
                        .then_inc(near_product.sem, 1)
                    return
                pool.wait_ge(*decay_ready.at(n, c * DECAYS + rung - 1))
                w = SPANS[rung - 1]
                nc.gpsimd.tensor_tensor(keys[:], at_chunk(k_, c), key_dec[:], ALU.mult)
                for kind, (first, count, _) in enumerate(KINDS):
                    last = nc.gpsimd.tensor_tensor(kind_cols(queries, w, kind), spans(at_chunk(q, c), w, first, count),
                                                   kind_cols(query_dec, w, kind), ALU.mult)
                last.then_inc(product_ready.sem, 1)

            def end_products(n, c):
                pool.wait_ge(*full(n, ("rung", c, RUNGS - 1, 1)))
                for e, tensor, decays in ((QUERY_DECAY, q, query_dec[:, :, 0:P]), (KEY_DECAY, k_, key_dec[:])):
                    pool.wait_ge(*decay_ready.at(n, c * DECAYS + e))
                    nc.gpsimd.tensor_tensor(at_chunk(tensor, c), at_chunk(tensor, c), decays, ALU.mult)\
                        .then_inc(product_ready.sem, 1)

            with pool.Fori(0, BLOCKS) as n:
                for f in range(2):
                    pool.wait_ge(*read(n, ("k", 2 + f)))
                def o_rsqrt(c):
                    pool.wait_ge(*o_ms_ready.at(n, c))
                    nc.gpsimd.tensor_tensor(o_rstd[:, c, :], o_ms[:, c, :], minus_half[:], ALU.pow)\
                        .then_inc(o_rstd_ready.sem, 1)

                def y_low(c, p):
                    pool.wait_ge(*y_hi_ready.at(n, p * TILES + c))
                    hi = at_chunk(h_hi[:, 4 * p:4 * p + 4, :].bitcast(F32), c)
                    nc.gpsimd.tensor_tensor(at_chunk(h_lo[:, 4 * p:4 * p + 4, :], c), heads_of(y_row(c)), hi,
                                            ALU.subtract).then_inc(mix_ready.sem, 1)

                for hs in range(STEPS):
                    c = hs // 4
                    rung_products(n, c, hs % 4)
                    if hs % 4 == 0 and c:
                        end_products(n, c - 1)
                    if hs in (10, 12, 14):
                        o_rsqrt(hs // 2 - 5)
                end_products(n, TILES - 1)
                o_rsqrt(TILES - 1)
                for p in range(2):
                    for c in range(TILES):
                        y_low(c, p)
                for which in range(3):
                    for t in range(TILES):
                        rsqrt(n, which, t)

        @block.scalar
        def _(act):
            def split_hi(n, i, slot, pair):
                act.wait_ge(*raw_loaded[slot].at(n, pair))
                act.wait_ge(*weights_used.at(n, i - 2))
                nc.scalar.activation(w_hi[:, slot, :], raw[:, slot, :], ACT.Copy).then_inc(hi_split.sem, 1)

            def square(which, t, source):
                nc.scalar.activation(hn[:, t, :], source[:, t, :], ACT.Square, accum_out=ssq[:, which, t:t + 1])\
                    .then_inc(ssq_ready.sem, 1)

            for tile, source in [(ident, identity), (gain_mem, norm_mem), (gain_mix, norm_mix)]:
                act.dma_start(tile[:], source).then_inc(first_consts_loaded, 16)
            act.wait_ge(mem_loaded, 16)
            for t in range(MT):
                square(0, t, xres)
            for copy in range(3 * PAIR // RANK):
                act.dma_start(w2_raw[copy * RANK:(copy + 1) * RANK], w_gate2).then_inc(w2_loaded, 16)

            def first_split_hi(i):
                act.wait_ge(*raw_loaded[i].early(0))
                nc.scalar.activation(w_hi[:, i, :], raw[:, i, :], ACT.Copy).then_inc(hi_split.sem, 1)

            first_split_hi(0)
            act.wait_ge(first_consts_loaded, 16 * 3)
            for k in range(KD):
                act.wait_ge(*early_full(("memT", k)))
                nc.scalar.activation(h_hi[:, k, 0:MEM], bank(("memT", k))[:, 0:MEM], ACT.Copy,
                                     scale=gain_mem[:, k:k + 1]).then_inc(hi_part.sem, 1)
            first_split_hi(1)
            act.wait_ge(*xin_loaded.early(0))
            for t in range(TILES):
                act.wait_ge(*normed.early(MT - 1))
                square(1, t, xin)
            for i in range(KV_CHUNKS):
                if i < 2:
                    for f in range(2):
                        h = 2 * i + f
                        act.wait_ge(*early_full(("km", h)))
                        nc.scalar.activation(kmT[:, h, :], bank(("km", h))[:, 0:MEM], ACT.Copy)\
                            .then_inc(bank_read[bank_of(("km", h))], 1)
                if i + 2 <= KV_CHUNKS:
                    act.wait_ge(*raw_loaded[i % 2].early((i + 2) // 2))
                    act.wait_ge(*weights_used.early(i))
                    nc.scalar.activation(w_hi[:, i % 2, :], raw[:, i % 2, :], ACT.Copy).then_inc(hi_split.sem, 1)
            act.wait_ge(consts_loaded, 16 * 7)
            act.wait_ge(w2_loaded, 16 * (3 * PAIR // RANK))
            nc.scalar.activation(w2_parts[:], w2_raw, ACT.Copy)
            nc.scalar.activation(wg_pair[:, :, 0:RANK], wg_raw, ACT.Copy).then_inc(wg_hi_ready, 1)
            for k in range(KD):
                act.wait_ge(*early_full(("x0T", k)))
                nc.scalar.activation(h_hi[:, k, :], bank(("x0T", k)), ACT.Copy,
                                     scale=gain_mix[:, k:k + 1]).then_inc(hi_part.sem, 1)

            with act.Fori(0, BLOCKS) as n:
                def next_chunk(i):
                    split_hi(n, i + 1, (i + 1) % 2, (i + 1) // 2)

                def copy_out(name, to, scale=1.0):
                    act.wait_ge(*full(n, name))
                    nc.scalar.activation(to, bank(name), ACT.Copy, scale=scale)\
                        .then_inc(bank_read[bank_of(name)], 1)

                def attention_exp(t):
                    for p in range(2):
                        act.wait_ge(*top_ready.at(n, 2 * t + p))
                        for h in (2 * p, 2 * p + 1):
                            last = nc.scalar.activation(
                                probs[:, t % 2, h * MEM:(h + 1) * MEM],
                                bank(("score", t, p))[:, (h % 2) * MEM:(h % 2 + 1) * MEM], ACT.Exp,
                                bias=neg_top[:, t, h:h + 1], scale=XSCALE, accum_out=den[:, t, h:h + 1])
                        last.then_inc(bank_read[bank_of(("score", t, p))], 1)

                def attention_probsT(t):
                    for p in range(2):
                        copy_out(("pT", t, p), probsT[:, t % 2, p * 512:(p + 1) * 512])

                def attention_hi(t):
                    for p in range(2):
                        act.wait_ge(*full(n, ("pv", t, p)))
                        nc.scalar.activation(at_chunk(mem_hi[:, 2 * p:2 * p + 2, :], t),
                                             heads_of(bank(("pv", t, p))[:, 0:2 * P], 2), ACT.Copy)\
                            .then_inc(hi_part.sem, 1)

                def near_decays(c):
                    act.wait_ge(*near_gap.at(n, c))
                    nc.scalar.activation(near_dec[:], near_dec[:], ACT.Exp, scale=1.0 / TAU).then_inc(near_decay.sem, 1)

                def rung_decays(c, rung):
                    act.wait_ge(*gap_ready.at(n, c * (DECAYS - 1) + rung - 1))
                    nc.scalar.activation(key_dec[:], key_dec[:], ACT.Exp, scale=1.0 / TAU)
                    nc.scalar.activation(query_dec[:], query_dec[:], ACT.Exp, scale=1.0 / TAU)\
                        .then_inc(decay_ready.sem, 1)

                def end_decays(c):
                    act.wait_ge(*product_ready.at(n, c * DECAYS + QUERY_DECAY - 1))
                    nc.scalar.activation(query_dec[:, :, 0:P], at_chunk(b_, c), ACT.Exp, scale=1.0 / TAU)\
                        .then_inc(decay_ready.sem, 1)
                    act.wait_ge(*gap_ready.at(n, c * (DECAYS - 1) + QUERY_DECAY))
                    nc.scalar.activation(key_dec[:], key_dec[:], ACT.Exp, scale=1.0 / TAU).then_inc(decay_ready.sem, 1)
                    nc.scalar.activation(chunk_decay[:, c, :], b_[:, :, (c + 1) * P - 1], ACT.Exp, scale=1.0 / TAU)\
                        .then_inc(chunk_decay_ready.sem, 1)

                next_chunk(0)
                for f in range(2):
                    copy_out(("xq", f), xq_a[:, f, :])
                act.wait_ge(*full(n, "g"))
                nc.scalar.activation(g_parts[2 * PAIR:3 * PAIR], bank("g")[0:PAIR, :], ACT.Copy)
                nc.scalar.activation(g_parts[0:PAIR], bank("g")[0:PAIR, :], ACT.Copy).then_inc(g_hi_ready.sem, 1)
                next_chunk(1)
                for f in range(2, 4):
                    copy_out(("xq", f), xq_a[:, f, :])
                act.wait_ge(*out_stored.at(n, -1))
                for h in range(HEADS):
                    act.wait_ge(*full(n, ("z", h)))
                    nc.scalar.activation(b_[:, h, :], bank(("z", h)), ACT.Identity, bias=gate_bias[:, h:h + 1])
                    nc.scalar.activation(soft[:, h, :], bank(("z", h)), ACT.Abs, bias=gate_bias[:, h:h + 1])\
                        .then_inc(bank_read[bank_of(("z", h))], 1)
                next_chunk(C_Q)
                for h in range(HEADS):
                    act.wait_ge(*read(n, ("z", h)))
                    last = nc.scalar.activation(soft[:, h, :], soft[:, h, :], ACT.Exp, scale=-1.0)
                last.then_inc(soft_exp.sem, 1)
                for f in range(2):
                    copy_out(("q", f), q[:, f, :], QSCALE)
                act.wait_ge(*soft_exp.at(n, 0))
                for h in range(HEADS):
                    nc.scalar.activation(soft[:, h, :], soft[:, h, :], ACT.Ln, bias=1.0).then_inc(soft_ready.sem, 1)
                next_chunk(C_Q + 1)
                attention_exp(0)
                for i in range(C_Q + 1, C_V):
                    if i > C_Q + 1:
                        next_chunk(i)
                    if i < C_K:
                        copy_out(("q", 2), q[:, 2, :], QSCALE)
                    if i - C_K >= 0:
                        attention_hi(i - C_K)
                    if i < C_K:
                        copy_out(("q", 3), q[:, 3, :], QSCALE)
                    attention_exp(i - C_Q)
                    attention_probsT(i - C_Q - 1)

                def o_square(c):
                    for h in range(HEADS):
                        act.wait_ge(*full(n, ("o", c, h // 2)))
                        last = nc.scalar.activation(
                            o_junk[:, h, :], bank(("o", c, h // 2))[:, (h % 2) * DV:(h % 2 + 1) * DV], ACT.Square,
                            accum_out=o_ssq[:, c, h:h + 1])
                    last.then_inc(o_ssq_ready.sem, 1)

                def o_norm(c):
                    act.wait_ge(*o_rstd_ready.at(n, c))
                    for h in range(HEADS):
                        ins = nc.scalar.activation(
                            o_n[c][:, h * DV:(h + 1) * DV],
                            bank(("o", c, h // 2))[:, (h % 2) * DV:(h % 2 + 1) * DV], ACT.Copy,
                            scale=o_rstd[:, c, h:h + 1])
                        if h % 2:
                            ins.then_inc(bank_read[bank_of(("o", c, h // 2))], 1)

                def keys_back(c):
                    act.wait_ge(*full(n, ("kT", c)))
                    nc.scalar.activation(at_chunk(k_, c), heads_of(bank(("kT", c))), ACT.Copy)\
                        .then_inc(bank_read[bank_of(("kT", c))], 1)

                def y_high(c, p):
                    act.wait_ge(*read(n, ("oT", c, p)))
                    nc.scalar.activation(at_chunk(h_hi[:, 4 * p:4 * p + 4, :], c), heads_of(y_row(c)), ACT.Copy)\
                        .then_inc(y_hi_ready.sem, 1)

                def gate_tanh(f):
                    act.wait_ge(*empty(n, ("r", f)))
                    act.wait_ge(*full(n, ("r", f)))
                    nc.scalar.activation(scratch[:, f % 2, :], bank(("r", f)), ACT.Tanh, scale=0.5)\
                        .then_inc(gate_tanh_ready.sem, 1)

                near_decays(0)
                rung_decays(0, 1)
                for hs in range(STEPS):
                    i, c = C_V + hs // 2, hs // 4
                    if hs in (9, 11, 13):
                        keys_back(hs // 2 - 4)
                    if hs in (11, 13, 15):
                        o_norm(hs // 2 - 5)
                    if hs % 2 == 0:
                        next_chunk(i)
                    if hs == 0:
                        attention_probsT(TILES - 1)
                    if hs in (1, 3):
                        attention_hi(2 + hs // 2)
                    before = hs - 1
                    if 0 <= before < 8 and before // 2 % 2 == 1:
                        d = before // 4
                        for t in (2 * (before % 2), 2 * (before % 2) + 1):
                            copy_out(("v", d, t), v[:, t, 512 * d:512 * (d + 1)])
                    if hs in (10, 12, 14):
                        o_square(hs // 2 - 5)
                    if hs >= 9:
                        gate_tanh(hs - 9)
                    if hs % 4 == 3:
                        end_decays(c)
                    elif hs:
                        rung_decays(c, hs % 4 + 1)
                    if hs % 4 == 1 and c + 1 < TILES:
                        near_decays(c + 1)

                gate_tanh(KD - 1)
                next_chunk(C_OUT)
                o_square(TILES - 1)
                keys_back(TILES - 1)
                for c in range(TILES - 1):
                    if c == 1:
                        o_norm(TILES - 1)
                    y_high(c, 0)
                y_high(TILES - 1, 0)
                next_chunk(C_OUT + 1)
                for c in range(TILES):
                    y_high(c, 1)

                def h_high(h, g):
                    act.wait_ge(*full(n, ("hT", h, g)))
                    for j in range(2):
                        last = nc.scalar.activation(h_hi[:, 2 * g + j, h * 256:(h + 1) * 256],
                                                    bank(("hT", h, g))[:, j * 256:(j + 1) * 256], ACT.Copy,
                                                    scale=gain_mlp[:, 2 * g + j:2 * g + j + 1])
                    last.then_inc(hi_part.sem, 1)

                for i in range(C_OUT + 2, C_UP[0]):
                    next_chunk(i)
                for t in range(TILES):
                    if t == TILES - 1:
                        h_high(0, 0)
                        h_high(0, 1)
                    act.wait_ge(*read(n, ("out", 1, t)))
                    square(0, t, xres)
                for h, g in [(0, 2), (0, 3), (1, 0), (1, 1), (1, 2), (1, 3)]:
                    h_high(h, g)

                for half in range(2):
                    with act.Fori(0, UF // 4) as j:
                        for c in range(2):
                            i = C_UP[half] + c
                            split_hi(n, j * 2 + (i + 1), (i + 1) % 2, j + (i + 1) // 2)
                            for f in range(2):
                                e = j * 4 + (half * UF + 2 * c + f)
                                act.wait_ge(*full(n, ("up", half, c, f), j * 2))
                                act.wait_ge(*u_ready.at(n, e - 2))
                                nc.scalar.activation(scratch[:, f, :], banks[:, f, :], ACT.Relu)\
                                    .then_inc(bank_read[f], 1)
                                act.wait_ge(*read(n, ("up", half, c, f), j * 2))
                                nc.scalar.activation(scratch[:, f, :], scratch[:, f, :], ACT.Square)\
                                    .then_inc(square_ready.sem, 1)
                    with act.Fori(0, 2) as d:
                        for kg in range(UF // KG):
                            i = C_DOWN[half] + kg
                            split_hi(n, d * 4 + (i + 1), (i + 1) % 2, d * 2 + (i + 1) // 2)
                            if half == 1:
                                act.wait_ge(*full(n, ("xT", kg), d * 2))
                                nc.scalar.activation(h_hi[:, bass.ds(d * 4 + kg, 1), :],
                                                     banks[:, 6 + kg % 2:7 + kg % 2, :], ACT.Copy,
                                                     scale=gain_mix[:, bass.ds(d * 4 + kg, 1)])\
                                    .then_inc(hi_part.sem, 1)
                    if half == 0:
                        act.wait_ge(*xin_loaded.at(n, 0))
                        act.wait_ge(*full(n, ("down", 0, 1, TILES - 1)))
                        for t in range(TILES):
                            square(1, t, xin)
                for t in range(TILES):
                    act.wait_ge(*read(n, ("down", 1, 1, t)))
                    square(2, t, xres)
                out_tile = act.snap(n * TILES)
                for t in range(TILES):
                    act.wait_ge(*out_ready.at(n, t))
                    act.dma_start(out_tiles[:, bass.ds(out_tile + t, 1), :], xres[:, t:t + 1, :])\
                        .then_inc(out_stored.sem, 16)
            act.wait_ge(*out_stored.at(BLOCKS - 1, TILES - 1))

        @block.vector
        def _(dve):
            steps = [0]

            def link(ins):
                steps[0] += 1
                ins.then_inc(dve_step, 1)
                dve.wait_ge(dve_step, steps[0])

            def restart():
                dve.sem_clear(dve_step)
                steps[0] = 0

            def split_lo(n, i, slot):
                dve.wait_ge(*hi_split.at(n, i))
                nc.vector.tensor_tensor(w_lo[:, slot, :], raw[:, slot, :], w_hi[:, slot, :].bitcast(F32),
                                        ALU.subtract).then_inc(lo_split.sem, 1)

            def mean_square(which, t):
                nc.vector.tensor_scalar(ms[:, which, t:t + 1], ssq[:, which, t:t + 1], 1.0 / D, EPS,
                                        ALU.mult, ALU.add).then_inc(ms_ready.sem, 1)

            def scale_tile(which, t, source, to):
                nc.vector.tensor_scalar(to[:, t, :], source[:, t, :], rstd[:, which, t:t + 1], None,
                                        ALU.mult).then_inc(normed.sem, 1)

            def low(name, k, gain, cols=BLOCK):
                nc.vector.scalar_tensor_tensor(
                    out=h_lo[:, k, 0:cols], in0=bank((name, k))[:, 0:cols], scalar=gain[:, k:k + 1],
                    in1=h_hi[:, k, 0:cols].bitcast(F32), op0=ALU.mult, op1=ALU.subtract)\
                    .then_inc(bank_read[bank_of((name, k))], 1)

            nc.vector.memset(carried_state[:], 0.0).then_inc(u_ready.sem, 2)
            nc.vector.nop().then_inc(out_stored.sem, 16)
            for t in range(MT):
                dve.wait_ge(*ssq_ready.early(t))
                mean_square(0, t)
            for t in range(MT):
                dve.wait_ge(*rstd_ready.early(t))
                scale_tile(0, t, xres, xres)

            def first_split_lo(i):
                dve.wait_ge(*hi_split.early(i))
                nc.vector.tensor_tensor(w_lo[:, i, :], raw[:, i, :], w_hi[:, i, :].bitcast(F32),
                                        ALU.subtract).then_inc(lo_split.sem, 1)

            first_split_lo(0)
            dve.wait_ge(first_consts_loaded, 16 * 3)
            for k in range(KD):
                dve.wait_ge(*hi_part.early(k))
                low("memT", k, gain_mem, MEM)
            first_split_lo(1)
            for t in range(TILES):
                dve.wait_ge(*ssq_ready.early(MT + t))
                mean_square(1, t)
            for t in range(TILES):
                dve.wait_ge(*rstd_ready.early(MT + t))
                scale_tile(1, t, xin, xin)
            for i in range(KV_CHUNKS):
                if i >= 2:
                    for m in range(MT):
                        name = ("vm", i - 2, m)
                        dve.wait_ge(*early_full(name))
                        nc.vector.tensor_copy(vm[:, m, (i - 2) * FCOLS:(i - 1) * FCOLS], bank(name)[:, 0:FCOLS])\
                            .then_inc(bank_read[bank_of(name)], 1)
                if i + 2 <= KV_CHUNKS:
                    dve.wait_ge(*hi_split.early(i + 2))
                    nc.vector.tensor_tensor(w_lo[:, i % 2, :], raw[:, i % 2, :], w_hi[:, i % 2, :].bitcast(F32),
                                            ALU.subtract).then_inc(lo_split.sem, 1)
            dve.wait_ge(consts_loaded, 16 * 7)
            nc.vector.tensor_copy(masks[:], masks_raw)
            nc.vector.tensor_copy(scanm[:], scan_raw)
            nc.vector.tensor_scalar(half_gain_o[:], gain_o[:], 0.5, None, ALU.mult).then_inc(half_gain_ready, 1)
            dve.wait_ge(wg_hi_ready, 1)
            nc.vector.tensor_tensor(w2_parts[2 * PAIR:], w2_raw[2 * PAIR:], w2_parts[2 * PAIR:].bitcast(F32),
                                    ALU.subtract)
            nc.vector.tensor_tensor(wg_pair[:, :, RANK:], wg_raw, wg_pair[:, :, 0:RANK].bitcast(F32),
                                    ALU.subtract).then_inc(wg_ready, 1)
            for k in range(KD):
                dve.wait_ge(*hi_part.early(KD + k))
                low("x0T", k, gain_mix)

            dve.wait_ge(half_gain_ready, 1)
            with dve.Fori(0, BLOCKS) as n:
                def next_chunk(i):
                    split_lo(n, i + 1, (i + 1) % 2)

                def attention_top(t):
                    for p in range(2):
                        dve.wait_ge(*full(n, ("score", t, p)))
                        link(nc.vector.reduce_max(top[:, t, 2 * p:2 * p + 2],
                                                  heads_of(bank(("score", t, p)), 2), AX_X))
                        nc.vector.tensor_scalar(neg_top[:, t, 2 * p:2 * p + 2], top[:, t, 2 * p:2 * p + 2],
                                                -XSCALE, None, ALU.mult).then_inc(top_ready.sem, 1)

                def attention_norm(t):
                    for p in range(2):
                        dve.wait_ge(*read(n, ("score", t, p)))
                        link(nc.vector.reciprocal(rden[:, t, 2 * p:2 * p + 2], den[:, t, 2 * p:2 * p + 2]))
                        for h in (2 * p, 2 * p + 1):
                            row = probs[:, t % 2, h * MEM:(h + 1) * MEM]
                            last = nc.vector.tensor_scalar(row, row, rden[:, t, h:h + 1], None, ALU.mult)
                        last.then_inc(probs_ready.sem, 1)

                def attention_low(t):
                    for p in range(2):
                        dve.wait_ge(*hi_part.at(n, 2 * t + p))
                        nc.vector.tensor_tensor(
                            at_chunk(mem_lo[:, 2 * p:2 * p + 2, :], t), heads_of(bank(("pv", t, p))[:, 0:2 * P], 2),
                            at_chunk(mem_hi[:, 2 * p:2 * p + 2, :].bitcast(F32), t), ALU.subtract)\
                            .then_inc(bank_read[bank_of(("pv", t, p))], 1)

                def copy_k(f):
                    dve.wait_ge(*full(n, ("k", f)))
                    nc.vector.tensor_copy(k_[:, f, :], bank(("k", f))).then_inc(bank_read[bank_of(("k", f))], 1)

                def near_gaps(c):
                    if c:
                        dve.wait_ge(*near_product.at(n, c - 1))
                    b = at_chunk(b_, c)
                    nc.vector.tensor_tensor(near_dec[:], odd(b), even(b), ALU.subtract).then_inc(near_gap.sem, 1)

                def rung_gaps(c, rung):
                    e, w, b = c * DECAYS + rung - 1, SPANS[rung - 1], at_chunk(b_, c)
                    if e:
                        dve.wait_ge(*product_ready.at(n, e - 1))
                    each = "p h (m w) -> p h m w"
                    nc.vector.tensor_tensor(
                        key_dec[:].rearrange(each, w=w),
                        b.rearrange(each, w=w)[:, :, :, w - 1:w].broadcast_to([P, HEADS, P // w, w]),
                        b.rearrange(each, w=w), ALU.subtract)
                    for kind, (first, count, _) in enumerate(KINDS):
                        last = nc.vector.tensor_tensor(kind_cols(query_dec, w, kind), spans(b, w, first, count),
                                                       span_end(b, w, first - 1, count), ALU.subtract)
                    last.then_inc(gap_ready.sem, 1)

                def plain_queries(c):
                    nc.vector.tensor_copy(queries[:, :, 0:P], at_chunk(q, c)).then_inc(plain_ready.sem, 1)

                def end_gap(c):
                    b = at_chunk(b_, c)
                    dve.wait_ge(*product_ready.at(n, c * DECAYS + QUERY_DECAY - 1))
                    nc.vector.tensor_tensor(key_dec[:], b[:, :, P - 1:P].broadcast_to([P, HEADS, P]), b,
                                            ALU.subtract).then_inc(gap_ready.sem, 1)

                def silu(f):
                    name, row = ("r", f), scratch[:, f % 2, :]
                    dve.wait_ge(*gate_tanh_ready.at(n, f))
                    link(nc.vector.tensor_scalar(row, row, 1.0, half_gain_o[:, f % 2:f % 2 + 1], ALU.add, ALU.mult))
                    nc.vector.tensor_tensor(sr[:, f, :], bank(name), row, ALU.mult)\
                        .then_inc(bank_read[bank_of(name)], 1)

                def take_rung(c, rung):
                    attention = heads_of(xq_a[:, c, :])
                    pairs = [(attention[:, 2 * p:2 * p + 2],
                              heads_of(bank(("rung", c, rung, p))[:, 0:2 * COLS], 2)) for p in range(2)]
                    for p in range(2):
                        dve.wait_ge(*full(n, ("rung", c, rung, p)))
                        if p == 0:
                            link(nc.vector.nop())
                    if rung == NEAR:
                        mask = masks[:, (RUNGS - 1) * COLS:].unsqueeze(1).broadcast_to([P, 2, ODD])
                        for p, (to, source) in enumerate(pairs):
                            link(nc.vector.tensor_tensor(to, source[:, :, 0:P],
                                                         ident[:].unsqueeze(1).broadcast_to([P, 2, P]), ALU.mult))
                            nc.vector.copy_predicated(odd(to), mask, source[:, :, P:COLS])\
                                .then_inc(bank_read[bank_of(("rung", c, rung, p))], 1)
                        return
                    w, base = SPANS[rung - 1], (rung - 1) * COLS
                    for kind, (first, count, col) in enumerate(KINDS):
                        at = slice(base + col, base + col + 32 * count)
                        mask = masks[:, at].unsqueeze(1).broadcast_to([P, 2, 32 * count])\
                            .rearrange("p h (g x) -> p h g x", x=count * w)
                        for p, (to, source) in enumerate(pairs):
                            ins = nc.vector.copy_predicated(spans(to, w, first, count), mask, kind_cols(source, w, kind))
                            if kind == len(KINDS) - 1:
                                ins.then_inc(bank_read[bank_of(("rung", c, rung, p))], 1)
                            elif p == 1:
                                link(ins)

                next_chunk(0)
                dve.wait_ge(*g_hi_ready.at(n, 0))
                nc.vector.tensor_tensor(g_parts[PAIR:2 * PAIR], bank("g")[0:PAIR, :], g_parts[0:PAIR].bitcast(F32),
                                        ALU.subtract).then_inc(bank_read[bank_of("g")], 1)
                next_chunk(1)
                next_chunk(C_Q)
                for h in range(HEADS):
                    dve.wait_ge(*soft_ready.at(n, h))
                    link(nc.vector.scalar_tensor_tensor(out=soft[:, h, :], in0=b_[:, h, :], scalar=0.0,
                                                        in1=soft[:, h, :], op0=ALU.min, op1=ALU.subtract))
                    last = nc.vector.tensor_tensor_scan(b_[:, h, :], scanm[:], soft[:, h, :], 0.0,
                                                        ALU.mult, ALU.add)
                last.then_inc(b_ready.sem, 1)
                dve.wait_ge(*b_ready.at(n, 0))
                attention_top(0)
                next_chunk(C_Q + 1)
                attention_norm(0)
                for i in range(C_Q + 1, C_V):
                    if i > C_Q + 1:
                        next_chunk(i)
                    if i >= C_K:
                        copy_k(2 * (i - C_K))
                        attention_low(i - C_K)
                        copy_k(2 * (i - C_K) + 1)
                    attention_top(i - C_Q)
                    attention_norm(i - C_Q)

                def update_state(c):
                    dve.wait_ge(*chunk_decay_ready.at(n, c))
                    if c:
                        dve.wait_ge(*full(n, ("o", c - 1, 1)))
                        dve.wait_ge(*read(n, ("su", c - 1, 1)))
                    for p in range(2):
                        dve.wait_ge(*full(n, ("su", c, p)))
                        for h in (2 * p, 2 * p + 1):
                            last = nc.vector.scalar_tensor_tensor(
                                out=states[(c + 1) % 2][:, h, :], in0=states[c % 2][:, h, :],
                                scalar=chunk_decay[:, c, h:h + 1],
                                in1=bank(("su", c, p))[:, (h % 2) * DV:(h % 2 + 1) * DV],
                                op0=ALU.mult, op1=ALU.add)
                        last.then_inc(bank_read[bank_of(("su", c, p))], 1)

                def o_mean_square(c):
                    dve.wait_ge(*o_ssq_ready.at(n, c))
                    nc.vector.tensor_scalar(o_ms[:, c, :], o_ssq[:, c, :], 1.0 / DV, EPS, ALU.mult, ALU.add)\
                        .then_inc(o_ms_ready.sem, 1)

                def gate_output(c, p):
                    dve.wait_ge(*full(n, ("oT", c, p)))
                    if p:
                        dve.wait_ge(*mix_ready.at(n, c))
                    nc.vector.tensor_tensor(heads_of(y_row(c)), heads_of(bank(("oT", c, p))),
                                            at_chunk(sr[:, 4 * p:4 * p + 4, :], c), ALU.mult)\
                        .then_inc(bank_read[bank_of(("oT", c, p))], 1)

                for f in range(2):
                    dve.wait_ge(*read(n, ("q", 2 + f)))
                plain_queries(0)
                near_gaps(0)
                rung_gaps(0, 1)
                for hs in range(STEPS):
                    i, c = C_V + hs // 2, hs // 4
                    if hs:
                        take_rung((hs - 1) // 4, (hs - 1) % 4)
                    if hs % 4 == 0 and c:
                        plain_queries(c)
                    if hs % 2 == 0:
                        next_chunk(i)
                    elif hs >= 9:
                        silu(hs - 9)
                    if hs in (1, 3):
                        attention_low(2 + hs // 2)
                    if hs % 4 == 3:
                        end_gap(c)
                    elif hs:
                        rung_gaps(c, hs % 4 + 1)
                    if hs % 4 == 1 and c + 1 < TILES:
                        near_gaps(c + 1)
                    if hs in (10, 12, 14):
                        silu(hs - 9)
                        update_state(hs // 2 - 5)
                        o_mean_square(hs // 2 - 5)

                take_rung(TILES - 1, RUNGS - 1)
                silu(KD - 1)
                next_chunk(C_OUT)
                o_mean_square(TILES - 1)
                for c in range(TILES):
                    gate_output(c, 0)
                next_chunk(C_OUT + 1)
                update_state(TILES - 1)
                for c in range(TILES):
                    gate_output(c, 1)

                def add_out(name, t, cols, more=0):
                    dve.wait_ge(*full(n, name, more))
                    nc.vector.tensor_tensor(xres[:, t, cols], bank(name), xres[:, t, cols], ALU.add)\
                        .then_inc(bank_read[bank_of(name)], 1)

                def norm_ms(which, t):
                    dve.wait_ge(*ssq_ready.at(n, which * TILES + t))
                    mean_square(which, t)

                def norm_scale(which, t, source, to):
                    dve.wait_ge(*rstd_ready.at(n, which * TILES + t))
                    scale_tile(which, t, source, to)

                def h_low(h, g):
                    dve.wait_ge(*hi_part.at(n, 2 * TILES + h * (KD // 2) + g))
                    for j in range(2):
                        at, part = slice(h * 256, (h + 1) * 256), slice(j * 256, (j + 1) * 256)
                        last = nc.vector.scalar_tensor_tensor(
                            out=h_lo[:, 2 * g + j, at], in0=bank(("hT", h, g))[:, part],
                            scalar=gain_mlp[:, 2 * g + j:2 * g + j + 1], in1=h_hi[:, 2 * g + j, at].bitcast(F32),
                            op0=ALU.mult, op1=ALU.subtract)
                    last.then_inc(bank_read[bank_of(("hT", h, g))], 1)

                for i in range(C_OUT + 2, C_UP[0]):
                    next_chunk(i)
                    if i == C_OUT + 2:
                        dve.wait_ge(*xres_loaded.at(n, 0))
                        for t in range(TILES):
                            add_out(("out", 0, t), t, slice(0, 512))
                second = slice(512, 1024)
                add_out(("out", 1, 0), 0, second)
                norm_ms(0, 0)
                for t in range(1, TILES):
                    add_out(("out", 1, t), t, second)
                    norm_scale(0, t - 1, xres, hn)
                    if t < TILES - 1:
                        norm_ms(0, t)
                h_low(0, 0)
                h_low(0, 1)
                norm_ms(0, TILES - 1)
                h_low(0, 2)
                norm_scale(0, TILES - 1, xres, hn)
                h_low(0, 3)
                for g in range(KD // 2):
                    h_low(1, g)
                restart()

                def final_scale(t):
                    dve.wait_ge(*rstd_ready.at(n, 2 * TILES + t))
                    nc.vector.scalar_tensor_tensor(out=xres[:, t, :], in0=xres[:, t, :], scalar=rstd[:, 2, t:t + 1],
                                                   in1=gain_fin[:], op0=ALU.mult, op1=ALU.mult)\
                        .then_inc(out_ready.sem, 1)

                for half in range(2):
                    with dve.Fori(0, UF // 4) as j:
                        for c in range(2):
                            i = C_UP[half] + c
                            split_lo(n, j * 2 + (i + 1), (i + 1) % 2)
                            for f in range(2):
                                at = bass.ds(j * 4 + (2 * c + f), 1)
                                dve.wait_ge(*square_ready.at(n, j * 4 + (half * UF + 2 * c + f)))
                                row = scratch[:, f:f + 1, :]
                                link(nc.vector.tensor_copy(u_hi[:, at, :], row))
                                nc.vector.tensor_tensor(u_lo[:, at, :], row, u_hi[:, at, :].bitcast(F32),
                                                        ALU.subtract).then_inc(u_ready.sem, 1)
                        restart()
                    if half == 0:
                        with dve.Fori(0, 2) as d:
                            for kg in range(UF // KG):
                                i = C_DOWN[0] + kg
                                split_lo(n, d * 4 + (i + 1), (i + 1) % 2)
                            for t in range(TILES):
                                add_out(("down", 0, 0, t), t, bass.ds(d * 512, 512), d)
                        for t in range(TILES):
                            norm_ms(1, t)
                        for t in range(TILES):
                            norm_scale(1, t, xin, xin)
                    else:
                        for d in range(2):
                            for kg in range(UF // KG):
                                i = C_DOWN[1] + 4 * d + kg
                                split_lo(n, i + 1, (i + 1) % 2)
                                k = 4 * d + kg
                                dve.wait_ge(*hi_part.at(n, 2 * TILES + KD + k))
                                low("xT", k, gain_mix)
                            for t in range(TILES):
                                add_out(("down", 1, d, t), t, slice(512 * d, 512 * (d + 1)))
                                if d == 1:
                                    if t >= 1:
                                        norm_ms(2, t - 1)
                                    if t >= 2:
                                        final_scale(t - 2)
                        norm_ms(2, TILES - 1)
                        final_scale(TILES - 2)
                        final_scale(TILES - 1)

        @block.tensor
        def _(pe):
            chunk_done = [False]

            def after_chunk(ins):
                if chunk_done[0]:
                    ins.then_inc(weights_used.sem, 1)
                chunk_done[0] = False

            def product(to, left, right, start, stop):
                after_chunk(pe.matmul(to, left[0], right[0], start=start, stop=False))
                pe.matmul(to, left[0], right[1], start=False, stop=False)
                return pe.matmul(to, left[1], right[0], start=False, stop=stop)

            def wait_weights(n, i):
                pe.wait_ge(*hi_split.at(n, i))
                pe.wait_ge(*lo_split.at(n, i))

            def feature_rows(slot, f, to, cols, ready=None):
                wh, wl = as_kblocks(w_hi, slot, KD), as_kblocks(w_lo, slot, KD)
                for k in range(KD):
                    if ready:
                        ready(k)
                    last = product(to, (wh[:, k, f * P:(f + 1) * P], wl[:, k, f * P:(f + 1) * P]),
                                   (h_hi[:, k, 0:cols], h_lo[:, k, 0:cols]), k == 0, k == KD - 1)
                return last

            def token_rows(slot, to, left, start, stop):
                wh, wl = as_kblocks(w_hi, slot, KG), as_kblocks(w_lo, slot, KG)
                for k in range(KG):
                    last = product(to, left(k), (wh[:, k, :], wl[:, k, :]), start and k == 0, stop and k == KG - 1)
                return last

            def transposes(name, source, tiles, k):
                for t in range(tiles):
                    last = pe.transpose(banks[:, bank_of((name, k)), t * P:(t + 1) * P],
                                        source[:, t, k * P:(k + 1) * P], ident[:])
                last.then_inc(bank_full[bank_of((name, k))], 1)

            pe.wait_ge(first_consts_loaded, 16 * 3)
            pe.wait_ge(*normed.early(MT - 1))
            for k in range(KD):
                if k >= len(EARLY_RING):
                    pe.wait_ge(*early_empty(("memT", k)))
                transposes("memT", xres, MT, k)
            for i in range(KV_CHUNKS):
                pe.wait_ge(*hi_split.early(i))
                pe.wait_ge(*lo_split.early(i))
                if i < 2:
                    for f in range(2):
                        name = ("km", 2 * i + f)
                        if i:
                            pe.wait_ge(*early_empty(name))
                        ready = (lambda k: pe.wait_ge(*early_read(("memT", k)))) if i == 0 and f == 0 else None
                        feature_rows(i % 2, f, bank(name)[:, 0:MEM], MEM, ready)\
                            .then_inc(bank_full[bank_of(name)], 1)
                else:
                    wh, wl = as_kblocks(w_hi, i % 2, KD), as_kblocks(w_lo, i % 2, KD)
                    for m in range(MT):
                        name = ("vm", i - 2, m)
                        if i == 3:
                            pe.wait_ge(*early_empty(name))
                        for k in range(KD):
                            at = slice(m * P, (m + 1) * P)
                            last = product(bank(name)[:, 0:FCOLS], (h_hi[:, k, at], h_lo[:, k, at]),
                                           (wh[:, k, :], wl[:, k, :]), k == 0, k == KD - 1)
                        last.then_inc(bank_full[bank_of(name)], 1)
                chunk_done[0] = True
            pe.wait_ge(*normed.early(MT + TILES - 1))
            for k in range(KD):
                pe.wait_ge(*early_empty(("x0T", k)))
                transposes("x0T", xin, TILES, k)
            for k in range(KD - len(EARLY_RING), KD):
                pe.wait_ge(*early_read(("x0T", k)))
            pe.wait_ge(wg_ready, 1)

            with pe.Fori(0, BLOCKS) as n:
                def feature_part(i, f, name):
                    if f == 0:
                        wait_weights(n, i)
                    pe.wait_ge(*empty(n, name))
                    feature_rows(i % 2, f, bank(name), BLOCK).then_inc(bank_full[bank_of(name)], 1)
                    chunk_done[0] = f == 1

                def gate_features():
                    pe.wait_ge(*empty(n, "g"))
                    for k in range(KD):
                        after_chunk(pe.matmul(bank("g")[0:PAIR, :], wg_pair[:, k, :], h_hi[:, k, :],
                                              start=k == 0, stop=False))
                        last = pe.matmul(bank("g")[0:PAIR, :], wg_pair[:, k, :], h_lo[:, k, :],
                                         start=False, stop=k == KD - 1)
                    last.then_inc(bank_full[bank_of("g")], 1)

                def gate_logits():
                    pe.wait_ge(*read(n, "g"))
                    for h in range(HEADS):
                        pe.wait_ge(*empty(n, ("z", h)))
                        pe.matmul(bank(("z", h)), w2_parts[:, h * DK:(h + 1) * DK], g_parts, start=True, stop=True)\
                            .then_inc(bank_full[bank_of(("z", h))], 1)

                def scores(t):
                    for p in range(2):
                        pe.wait_ge(*empty(n, ("score", t, p)))
                        if t == 0:
                            for h in (2 * p, 2 * p + 1):
                                pe.wait_ge(*read(n, ("xq", h)))
                        for h in (2 * p, 2 * p + 1):
                            last = pe.matmul(bank(("score", t, p))[:, (h % 2) * MEM:(h % 2 + 1) * MEM],
                                             xq_a[:, h, t * P:(t + 1) * P], kmT[:, h, :], start=True, stop=True)
                            if h == 0:
                                after_chunk(last)
                        last.then_inc(bank_full[bank_of(("score", t, p))], 1)

                def probs_transposes(t):
                    for p in range(2):
                        name = ("pT", t, p)
                        pe.wait_ge(*empty(n, name))
                        pe.wait_ge(*probs_ready.at(n, 2 * t + p))
                        for j in range(4):
                            at = (4 * p + j) * P
                            last = pe.transpose(bank(name)[:, j * P:(j + 1) * P], probs[:, t % 2, at:at + P], ident[:])
                        last.then_inc(bank_full[bank_of(name)], 1)

                def attention_values(t):
                    for p in range(2):
                        name = ("pv", t, p)
                        pe.wait_ge(*empty(n, name))
                        pe.wait_ge(*read(n, ("pT", t, p)))
                        for h in (2 * p, 2 * p + 1):
                            for m in range(MT):
                                last = pe.matmul(bank(name)[:, (h % 2) * P:(h % 2 + 1) * P], vm[:, m, h * P:(h + 1) * P],
                                                 probsT[:, t % 2, (h * MT + m) * P:(h * MT + m + 1) * P],
                                                 start=m == 0, stop=m == MT - 1)
                        last.then_inc(bank_full[bank_of(name)], 1)

                def rung_scores(c, rung):
                    if rung == NEAR:
                        if c == 0:
                            for f in range(2):
                                pe.wait_ge(*read(n, ("k", 2 + f)))
                        pe.wait_ge(*plain_ready.at(n, c))
                        pe.wait_ge(*near_product.at(n, c))
                    else:
                        pe.wait_ge(*product_ready.at(n, c * DECAYS + rung - 1))
                    for p in range(2):
                        name = ("rung", c, rung, p)
                        pe.wait_ge(*empty(n, name))
                        for h in (2 * p, 2 * p + 1):
                            left = k_[:, h, c * P:(c + 1) * P] if rung == NEAR else keys[:, h, :]
                            ins = pe.matmul(bank(name)[:, (h % 2) * COLS:(h % 2 + 1) * COLS], left, queries[:, h, :],
                                            start=True, stop=True)
                            if h == 0:
                                after_chunk(ins)
                        ins.then_inc(bank_full[bank_of(name)], 1)

                def state_step(what, c):
                    if what == "kT":
                        name = ("kT", c)
                        pe.wait_ge(*empty(n, name))
                        pe.wait_ge(*product_ready.at(n, c * DECAYS + KEY_DECAY))
                        for h in range(HEADS):
                            last = pe.transpose(bank(name)[:, h * P:(h + 1) * P], k_[:, h, c * P:(c + 1) * P], ident[:])
                            if h == 0:
                                after_chunk(last)
                        last.then_inc(bank_full[bank_of(name)], 1)
                    elif what == "su":
                        pe.wait_ge(*read(n, ("kT", c)))
                        for p in range(2):
                            name = ("su", c, p)
                            pe.wait_ge(*empty(n, name))
                            pe.wait_ge(*read(n, ("v", p, c)))
                            for h in (2 * p, 2 * p + 1):
                                last = pe.matmul(bank(name)[:, (h % 2) * DV:(h % 2 + 1) * DV],
                                                 k_[:, h, c * P:(c + 1) * P], v[:, c, h * DV:(h + 1) * DV],
                                                 start=True, stop=True)
                            last.then_inc(bank_full[bank_of(name)], 1)
                    else:
                        for p in range(2):
                            pe.wait_ge(*read(n, ("rung", c, RUNGS - 1, p)))
                        pe.wait_ge(*product_ready.at(n, c * DECAYS + QUERY_DECAY))
                        for p in range(2):
                            name = ("o", c, p)
                            pe.wait_ge(*empty(n, name))
                            if c:
                                pe.wait_ge(*read(n, ("su", c - 1, p)))
                            for h in (2 * p, 2 * p + 1):
                                to = bank(name)[:, (h % 2) * DV:(h % 2 + 1) * DV]
                                pe.matmul(to, xq_a[:, c, h * P:(h + 1) * P], v[:, c, h * DV:(h + 1) * DV],
                                          start=True, stop=False)
                                last = pe.matmul(to, q[:, h, c * P:(c + 1) * P], states[c % 2][:, h, :],
                                                 start=False, stop=True)
                            last.then_inc(bank_full[bank_of(name)], 1)

                def output_transposes(c, p):
                    name = ("oT", c, p)
                    pe.wait_ge(*empty(n, name))
                    pe.wait_ge(*read(n, ("o", c, 1)))
                    if p == 0:
                        pe.wait_ge(*read(n, ("o", c, 0)))
                    for j in range(4):
                        at = (4 * p + j) * P
                        last = pe.transpose(bank(name)[:, j * P:(j + 1) * P], o_n[c][:, at:at + P], ident[:])
                        if j == 0:
                            after_chunk(last)
                    last.then_inc(bank_full[bank_of(name)], 1)

                def out_tile(i, t):
                    d, kg = (i - C_OUT) // 3, OUT_ORDER[(i - C_OUT) % 3]
                    name, at = ("out", d, t), slice(t * P, (t + 1) * P)
                    if t == 0:
                        wait_weights(n, i)
                    if kg == OUT_ORDER[0]:
                        pe.wait_ge(*empty(n, name))
                    hi, lo, k0 = (h_hi, h_lo, KG * kg) if kg < 2 else (mem_hi, mem_lo, 0)
                    last = token_rows(i % 2, bank(name), lambda k: (hi[:, k0 + k, at], lo[:, k0 + k, at]),
                                      kg == OUT_ORDER[0], kg == OUT_ORDER[2])
                    if kg == OUT_ORDER[2]:
                        last.then_inc(bank_full[bank_of(name)], 1)
                    chunk_done[0] = t == TILES - 1

                for b in (6, 7):
                    pe.wait_ge(bank_read[b], n * USES.count[b] + EARLY.count[b])
                feature_part(0, 0, ("xq", 0))
                feature_part(0, 1, ("xq", 1))
                gate_features()
                feature_part(1, 0, ("xq", 2))
                feature_part(1, 1, ("xq", 3))
                gate_logits()
                for i in range(C_Q, C_V):
                    for f in range(2):
                        feature_part(i, f, ("q", 2 * (i - C_Q) + f) if i < C_K else ("k", 2 * (i - C_K) + f))
                        if f == 0 and i >= C_K:
                            attention_values(i - C_K)
                    scores(i - C_Q)
                    if i > C_Q:
                        probs_transposes(i - C_Q - 1)
                for hs in range(STEPS):
                    i, f = C_V + hs // 2, hs % 2
                    if i < C_R:
                        d, kg = divmod(i - C_V, 2)
                        if f == 0:
                            wait_weights(n, i)
                        for t in (2 * f, 2 * f + 1):
                            if kg == 0:
                                pe.wait_ge(*empty(n, ("v", d, t)))
                            at = slice(t * P, (t + 1) * P)
                            last = token_rows(i % 2, bank(("v", d, t)),
                                              lambda k: (h_hi[:, KG * kg + k, at], h_lo[:, KG * kg + k, at]),
                                              kg == 0, kg == 1)
                            if kg == 1:
                                last.then_inc(bank_full[bank_of(("v", d, t))], 1)
                        chunk_done[0] = f == 1
                    else:
                        feature_part(i, f, ("r", hs - 8))
                    if hs == 0:
                        probs_transposes(TILES - 1)
                    if hs in (0, 2):
                        attention_values(2 + hs // 2)
                    rung_scores(hs // 4, hs % 4)
                    for what, c in STATE_STEPS.get(hs, ()):
                        state_step(what, c)

                for p in range(2):
                    pe.wait_ge(*read(n, ("pv", TILES - 1, p)))
                out_tile(C_OUT, 0)
                out_tile(C_OUT, 1)
                state_step("o", TILES - 1)
                state_step("kT", TILES - 1)
                out_tile(C_OUT, 2)
                for c in range(TILES - 1):
                    output_transposes(c, 0)
                out_tile(C_OUT, 3)
                output_transposes(TILES - 1, 0)
                state_step("su", TILES - 1)
                for t in range(TILES):
                    if t == 2:
                        for c in range(TILES):
                            output_transposes(c, 1)
                    pe.wait_ge(*mix_ready.at(n, t))
                    out_tile(C_OUT + 1, t)
                for t in range(TILES):
                    pe.wait_ge(*mix_ready.at(n, TILES + t))
                    out_tile(C_OUT + 2, t)
                for i in range(C_OUT + 3, C_UP[0]):
                    for t in range(TILES):
                        out_tile(i, t)

                def h_transposes(h):
                    pe.wait_ge(*normed.at(n, 2 * h + 1))
                    for g in range(KD // 2):
                        name = ("hT", h, g)
                        pe.wait_ge(*empty(n, name))
                        for j in range(2):
                            for t in range(2):
                                last = pe.transpose(bank(name)[:, (2 * j + t) * P:(2 * j + t + 1) * P],
                                                    hn[:, 2 * h + t, (2 * g + j) * P:(2 * g + j + 1) * P], ident[:])
                        last.then_inc(bank_full[bank_of(name)], 1)

                def up_chunk(half, c, j):
                    wait_weights(n, j * 2 + (C_UP[half] + c))
                    for f in range(2):
                        pe.wait_ge(*empty(n, ("up", half, c, f), j * 2))
                        feature_rows(c, f, banks[:, f, :], BLOCK).then_inc(bank_full[f], 1)
                    chunk_done[0] = True

                def down_columns(half, d):
                    for kg in range(UF // KG):
                        wait_weights(n, d * 4 + (C_DOWN[half] + kg))
                        pe.wait_ge(*u_ready.at(n, half * UF + KG * (kg + 1) - 1))
                        for t in range(TILES):
                            name, at = ("down", half, 0, t), slice(t * P, (t + 1) * P)
                            if kg == 0:
                                pe.wait_ge(*empty(n, name, d))
                            last = token_rows(kg % 2, bank(name),
                                              lambda k: (u_hi[:, KG * kg + k, at], u_lo[:, KG * kg + k, at]),
                                              kg == 0, kg == UF // KG - 1)
                            if kg == UF // KG - 1:
                                last.then_inc(bank_full[bank_of(name)], 1)
                            if half == 1 and t == 1:
                                pe.wait_ge(*normed.at(n, 2 * TILES - 1))
                                pe.wait_ge(*empty(n, ("xT", 4 * d + kg)))
                                transposes("xT", xin, TILES, 4 * d + kg)
                        chunk_done[0] = True

                h_transposes(0)
                wait_weights(n, C_UP[0])
                wh, wl = as_kblocks(w_hi, 0, KD), as_kblocks(w_lo, 0, KD)
                for h in range(2):
                    at = slice(h * 256, (h + 1) * 256)
                    for g in range(KD // 2):
                        if h == 0 and g == KD // 2 - 1:
                            h_transposes(1)
                        pe.wait_ge(*read(n, ("hT", h, g)))
                        for f in range(2):
                            if h == 0 and g == 0:
                                pe.wait_ge(*empty(n, ("up", 0, 0, f)))
                            for k in (2 * g, 2 * g + 1):
                                last = product(banks[:, f, at],
                                               (wh[:, k, f * P:(f + 1) * P], wl[:, k, f * P:(f + 1) * P]),
                                               (h_hi[:, k, at], h_lo[:, k, at]), k == 0, k == KD - 1)
                            if h == 1 and g == KD // 2 - 1:
                                last.then_inc(bank_full[f], 1)
                chunk_done[0] = True
                up_chunk(0, 1, 0)

                for half in range(2):
                    with pe.Fori(1 - half, UF // 4) as j:
                        for c in range(2):
                            up_chunk(half, c, j)
                    if half == 0:
                        with pe.Fori(0, 2) as d:
                            down_columns(0, d)
                    else:
                        for d in range(2):
                            down_columns(1, d)


IN_NAMES = ["x", "mem", "norm_mix", "norm_mem", "w_kv", "w_out", "norm_mlp", "w_up", "w_down", "gla_w_in",
            "gla_w_gate2", "gla_b_gate", "gla_out_gain", "final_norm"]

BY_PARTITION = ("norm_mix", "norm_mem", "norm_mlp", "gla_b_gate", "gla_out_gain")


def shape_constants():
    s = np.arange(P)[:, None]
    masks = []
    for w in SPANS:
        for first, count, _ in KINDS:
            t = np.arange(P).reshape(-1, 4 * w)[:, first * w:(first + count) * w].reshape(1, -1)
            masks.append((s // (4 * w) == t // (4 * w)) & (s // w % 4 == first - 1))
    t = np.arange(1, P, 2)[None, :]
    masks = np.concatenate(masks + [s == t - 1], axis=1).astype(np.float32)
    scan = np.ones((P, BLOCK), np.float32)
    scan[:, ::P] = 0
    return {"rung_masks": masks, "identity": np.eye(P, dtype=np.float32), "scan_mask": scan}


def kernel(**inputs):
    import concourse.bacc as bacc
    from concourse.bass_utils import run_bass_kernel_spmd

    nc = bacc.Bacc("TRN2", target_bir_lowering=False, num_devices=1)
    arrays, args = {}, []

    def give(name, a):
        a = np.ascontiguousarray(a)
        arrays[name] = a
        args.append(nc.dram_tensor(name, a.shape, mybir.dt.from_np(a.dtype), kind="ExternalInput").ap())

    for name in IN_NAMES:
        a = np.asarray(inputs[name])
        a = a if name == "final_norm" else a[0]
        if name in BY_PARTITION:
            a = a.reshape(-1, P).T
        give(f"in_{name}", a)
    for name, a in shape_constants().items():
        give(name, a)
    out = nc.dram_tensor("out", (SEQ, D), F32, kind="ExternalOutput").ap()
    build(nc, *args, out)
    r = run_bass_kernel_spmd(nc, [arrays], core_ids=[0])
    return r.results[0]["out"].reshape(1, SEQ, D)
```
